# Optimizing a Trainium2 kernel written in Bass

```python
import math
import jax, jax.numpy as jnp
from jax import lax
import numpy as np

D_MODEL = 4096
BATCH = 1
SEQ = 256
DEPTH = 1

A_HEADS = 16
A_KV_GROUPS = 4
A_HEADS_PER_GROUP = A_HEADS // A_KV_GROUPS
HEAD_DIM = 128
A_WIDTH = A_HEADS * HEAD_DIM
A_KV_WIDTH = A_KV_GROUPS * HEAD_DIM
L_CMP = 32
STRIDE_CMP = 16
L_SEL = 64
N_SEL = 16
WINDOW = 512
Q_BLOCK = 128
BIG = 1e9
B_GROUPS = 16
CHUNK = 128
B_WIDTH = 2048
B_GROUP_DIM = B_WIDTH // B_GROUPS
NUM_BUCKETS = 32
MAX_DISTANCE = 128
NORM_EPS = 1e-6
NEG_INF = -1e30
SPLIT_SIZES = (A_WIDTH, 6 * A_KV_WIDTH, 3 * A_HEADS, A_WIDTH, B_WIDTH, B_WIDTH, B_WIDTH, D_MODEL, D_MODEL)
IN_WIDTH = A_WIDTH + 6 * A_KV_WIDTH + 3 * A_HEADS + A_WIDTH + 3 * B_WIDTH + 2 * D_MODEL

kernel_name = "hybrid_nsa_gmlp_gated_parallel"

def rms_norm(x, g):
    xf = x.astype(jnp.float32)
    y = xf * lax.rsqrt(jnp.mean(xf * xf, axis=-1, keepdims=True) + NORM_EPS)
    return (y * g.astype(jnp.float32)).astype(x.dtype)

def masked_softmax(logits, mask):
    lf = jnp.where(mask, logits.astype(jnp.float32), NEG_INF)
    return jax.nn.softmax(lf, axis=-1)

def t5_bucket(dist):
    n = jnp.maximum(dist, 0)
    max_exact = NUM_BUCKETS // 2
    nf = jnp.maximum(n, 1).astype(jnp.float32)
    large = max_exact + (jnp.log(nf / max_exact) / math.log(MAX_DISTANCE / max_exact)
                         * (NUM_BUCKETS - max_exact)).astype(jnp.int32)
    large = jnp.minimum(large, NUM_BUCKETS - 1)
    return jnp.where(n < max_exact, n, large)

def compress(kv, pe, w1, w2):
    b, t, g, dh = kv.shape
    nc = (t - L_CMP) // STRIDE_CMP + 1
    idx = jnp.arange(nc)[:, None] * STRIDE_CMP + jnp.arange(L_CMP)[None, :]
    blk = kv[:, idx] + pe[None, None, :, None, :]
    blk = jnp.transpose(blk, (0, 1, 3, 2, 4)).reshape(b, nc, g, L_CMP * dh)
    return jax.nn.silu(blk @ w1) @ w2

def nsa_compressed(q, kc, vc, rel_bias, t_pos):
    b, t, g, r, dh = q.shape
    nc = kc.shape[1]
    blk_end = jnp.arange(nc, dtype=jnp.int32) * STRIDE_CMP + (L_CMP - 1)
    dist = t_pos[:, None] - blk_end[None, :]
    valid = dist >= 0
    bias = rel_bias[t5_bucket(dist)].reshape(t, nc, g, r).transpose(2, 3, 0, 1)
    s = jnp.einsum('btgrd,bngd->bgrtn', q, kc) * (dh ** -0.5) + bias
    any_valid = jnp.any(valid, axis=-1)[:, None].astype(jnp.float32)
    p = masked_softmax(s, valid) * any_valid
    o = jnp.einsum('bgrtn,bngd->btgrd', p.astype(vc.dtype), vc)
    return o, p

def select_blocks(p_cmp, t_pos):
    pg = p_cmp.sum(axis=2)
    nc = pg.shape[-1]
    t = t_pos.shape[0]
    ns = t // L_SEL
    m_rng = L_SEL // STRIDE_CMP
    n_rng = L_CMP // STRIDE_CMP
    offs = (jnp.arange(m_rng)[:, None] - jnp.arange(n_rng)[None, :]).reshape(-1)
    idx = m_rng * jnp.arange(ns)[:, None] + offs[None, :]
    ok = (idx >= 0) & (idx < nc)
    gathered = jnp.take(pg, jnp.clip(idx, 0, nc - 1), axis=-1)
    imp = jnp.where(ok, gathered, 0.0).sum(-1)
    jt = t_pos // L_SEL
    j = jnp.arange(ns, dtype=jnp.int32)[None, :]
    forced = (j == 0) | (j == jt[:, None]) | (j == jt[:, None] - 1)
    future = j > jt[:, None]
    score = jnp.where(forced, BIG, jnp.where(future, -1.0, imp))
    _, sel = lax.top_k(score, min(N_SEL, ns))
    return sel

def nsa_selected(q, ks, vs, sel, rel_bias, t_pos):
    b, t, g, r, dh = q.shape
    ns = t // L_SEL
    nq = t // Q_BLOCK
    n = sel.shape[-1]
    kb = ks.reshape(b, ns, L_SEL, g, dh).transpose(0, 3, 1, 2, 4)
    vb = vs.reshape(b, ns, L_SEL, g, dh).transpose(0, 3, 1, 2, 4)
    tbl = rel_bias.reshape(NUM_BUCKETS, g, r).transpose(1, 0, 2)
    qc = q.reshape(b, nq, Q_BLOCK, g, r, dh).transpose(1, 0, 2, 3, 4, 5)
    selc = sel.reshape(b, g, nq, Q_BLOCK, n).transpose(2, 0, 1, 3, 4)
    tc = t_pos.reshape(nq, Q_BLOCK)
    bi = jnp.arange(b)[:, None, None, None]
    gi = jnp.arange(g)[None, :, None, None]
    key_off = jnp.arange(L_SEL, dtype=jnp.int32)

    def block(args):
        q_b, sel_b, t_b = args
        kg = kb[bi, gi, sel_b]
        vg = vb[bi, gi, sel_b]
        pos = sel_b[..., None] * L_SEL + key_off
        dist = t_b[None, None, :, None, None] - pos
        bias = tbl[gi[..., None], t5_bucket(dist)]
        bias = jnp.moveaxis(bias, -1, 2).reshape(b, g, r, Q_BLOCK, n * L_SEL)
        s = jnp.einsum('bqgrd,bgqnld->bgrqnl', q_b, kg).reshape(b, g, r, Q_BLOCK, n * L_SEL)
        s = s * (dh ** -0.5) + bias
        valid = (dist >= 0).reshape(b, g, 1, Q_BLOCK, n * L_SEL)
        p = masked_softmax(s, valid).astype(vg.dtype)
        return jnp.einsum('bgrqk,bgqkd->bqgrd', p, vg.reshape(b, g, Q_BLOCK, n * L_SEL, dh))

    o = lax.map(block, (qc, selc, tc))
    return o.transpose(1, 0, 2, 3, 4, 5).reshape(b, t, g, r, dh)

def nsa_window(q, kw, vw, rel_bias, t_pos):
    b, t, g, r, dh = q.shape
    nb = t // Q_BLOCK
    nw = WINDOW // Q_BLOCK
    kk = (nw + 1) * Q_BLOCK
    pad = ((0, 0), (WINDOW, 0), (0, 0), (0, 0))
    kp = jnp.pad(kw, pad).reshape(b, nb + nw, Q_BLOCK, g, dh)
    vp = jnp.pad(vw, pad).reshape(b, nb + nw, Q_BLOCK, g, dh)
    blk = jnp.arange(nb)[:, None] + jnp.arange(nw + 1)[None, :]
    kband = kp[:, blk].reshape(b, nb, kk, g, dh)
    vband = vp[:, blk].reshape(b, nb, kk, g, dh)
    pos_k = ((blk - nw)[..., None] * Q_BLOCK + jnp.arange(Q_BLOCK)).reshape(nb, kk).astype(jnp.int32)
    t_q = t_pos.reshape(nb, Q_BLOCK)
    dist = t_q[:, :, None] - pos_k[:, None, :]
    valid = (dist >= 0) & (dist < WINDOW) & (pos_k >= 0)[:, None, :]
    bias = rel_bias[t5_bucket(dist)].reshape(nb, Q_BLOCK, kk, g, r).transpose(3, 4, 0, 1, 2)
    qb = q.reshape(b, nb, Q_BLOCK, g, r, dh)
    s = jnp.einsum('bnqgrd,bnkgd->bgrnqk', qb, kband) * (dh ** -0.5) + bias
    p = masked_softmax(s, valid).astype(vband.dtype)
    o = jnp.einsum('bgrnqk,bnkgd->bnqgrd', p, vband)
    return o.reshape(b, t, g, r, dh)

def gmlp_chunked(u, v, norm_g, w_s, b_s):
    b, t, _ = u.shape
    nc = t // CHUNK
    u = jax.nn.gelu(u)
    v = rms_norm(jax.nn.gelu(v), norm_g)
    vc = v.reshape(b, nc, CHUNK, B_GROUPS, B_GROUP_DIM)
    causal = jnp.tril(jnp.ones((CHUNK, CHUNK), dtype=bool))
    w = jnp.where(causal[None], w_s, 0)
    f = jnp.einsum('gpq,bcqgd->bcpgd', w, vc) + b_s.T[None, None, :, :, None]
    return u * f.reshape(b, t, B_WIDTH)

def setup_inputs(seed: int = 0) -> dict:
    key = jax.random.key(seed)
    ks = jax.random.split(key, 17)

    def nrm(k, shape, scale):
        return jax.random.normal(k, shape, jnp.float32) * scale

    lc = L_CMP * HEAD_DIM
    return {
        "x": nrm(ks[0], (BATCH, SEQ, D_MODEL), 1.0),
        "rel_bias": nrm(ks[1], (NUM_BUCKETS, A_HEADS), 0.5),
        "pre_norm": 1.0 + nrm(ks[2], (DEPTH, D_MODEL), 0.01),
        "w_in": nrm(ks[3], (DEPTH, D_MODEL, IN_WIDTH), D_MODEL ** -0.5),
        "cmp_pe_k": nrm(ks[4], (DEPTH, L_CMP, HEAD_DIM), 0.1),
        "cmp_w1_k": nrm(ks[5], (DEPTH, lc, HEAD_DIM), lc ** -0.5),
        "cmp_w2_k": nrm(ks[6], (DEPTH, HEAD_DIM, HEAD_DIM), HEAD_DIM ** -0.5),
        "cmp_pe_v": nrm(ks[7], (DEPTH, L_CMP, HEAD_DIM), 0.1),
        "cmp_w1_v": nrm(ks[8], (DEPTH, lc, HEAD_DIM), lc ** -0.5),
        "cmp_w2_v": nrm(ks[9], (DEPTH, HEAD_DIM, HEAD_DIM), HEAD_DIM ** -0.5),
        "w_out_a": nrm(ks[10], (DEPTH, A_WIDTH, D_MODEL), A_WIDTH ** -0.5),
        "sgu_norm": 1.0 + nrm(ks[11], (DEPTH, B_WIDTH), 0.01),
        "sgu_w": nrm(ks[12], (DEPTH, B_GROUPS, CHUNK, CHUNK), CHUNK ** -0.5),
        "sgu_b": 1.0 + nrm(ks[13], (DEPTH, B_GROUPS, CHUNK), 0.1),
        "w_out_b": nrm(ks[14], (DEPTH, B_WIDTH, D_MODEL), B_WIDTH ** -0.5),
        "w_out": nrm(ks[15], (DEPTH, D_MODEL, D_MODEL), D_MODEL ** -0.5),
        "post_norm": 1.0 + nrm(ks[16], (DEPTH, D_MODEL), 0.01),
    }

def reference(x, rel_bias, pre_norm, w_in, cmp_pe_k, cmp_w1_k, cmp_w2_k, cmp_pe_v,
              cmp_w1_v, cmp_w2_v, w_out_a, sgu_norm, sgu_w, sgu_b, w_out_b, w_out, post_norm):
    b, t, _ = x.shape
    g, r, dh = A_KV_GROUPS, A_HEADS_PER_GROUP, HEAD_DIM
    t_pos = jnp.arange(t, dtype=jnp.int32)
    offsets = [int(o) for o in np.cumsum(SPLIT_SIZES)[:-1]]
    for layer in range(DEPTH):
        h = rms_norm(x, pre_norm[layer])
        proj = h @ w_in[layer]
        q, kv, gates_a, z_a, u_b, v_b, z_b, m_a, m_b = jnp.split(proj, offsets, axis=-1)
        q = q.reshape(b, t, g, r, dh)
        kv = kv.reshape(b, t, 6, g, dh)
        kc = compress(kv[:, :, 0], cmp_pe_k[layer], cmp_w1_k[layer], cmp_w2_k[layer])
        vc = compress(kv[:, :, 1], cmp_pe_v[layer], cmp_w1_v[layer], cmp_w2_v[layer])
        o_cmp, p_cmp = nsa_compressed(q, kc, vc, rel_bias, t_pos)
        sel = select_blocks(p_cmp, t_pos)
        o_sel = nsa_selected(q, kv[:, :, 2], kv[:, :, 3], sel, rel_bias, t_pos)
        o_win = nsa_window(q, kv[:, :, 4], kv[:, :, 5], rel_bias, t_pos)
        ga = jax.nn.sigmoid(gates_a).reshape(b, t, g, r, 3)
        o_a = (ga[..., 0:1] * o_cmp + ga[..., 1:2] * o_sel + ga[..., 2:3] * o_win).reshape(b, t, A_WIDTH)
        y_a = (o_a * jax.nn.silu(z_a)) @ w_out_a[layer]
        o_b = gmlp_chunked(u_b, v_b, sgu_norm[layer], sgu_w[layer], sgu_b[layer])
        y_b = (o_b * jax.nn.silu(z_b)) @ w_out_b[layer]
        merged = jax.nn.sigmoid(m_a) * y_a + jax.nn.sigmoid(m_b) * y_b
        x = x + rms_norm(merged @ w_out[layer], post_norm[layer])
    return x


_drawn_inputs = setup_inputs


def setup_inputs(seed=0):
    import zlib

    import numpy as np

    out = dict(_drawn_inputs(seed))
    spreads = {}
    factors = {'pre_norm': 4.908, 'cmp_pe_k': 8.0, 'sgu_norm': 8.0, 'post_norm': 8.0}
    for name, (base, spread) in spreads.items():
        noise = np.random.default_rng([zlib.crc32(name.encode()), seed]).standard_normal(out[name].shape)
        drawn = base * np.exp(spread * noise) if base else spread * noise
        out[name] = __import__('jax').numpy.asarray(drawn.astype(out[name].dtype))
    for name, factor in factors.items():
        out[name] = (out[name] * factor).astype(out[name].dtype)
    return out
```

```python
from contextlib import ExitStack

import numpy as np
import concourse.bass as bass
from concourse import mybir

F32 = mybir.dt.float32
F32R = mybir.dt.float32r
ALU = mybir.AluOpType
ACT = mybir.ActivationFunctionType
AX = mybir.AxisListType
ds = bass.ds

P = 128
T = 256
NT = T // P
D = 4096
KD = D // P
HEADS, GROUPS, DH = 16, 4, 128
AW = HEADS * DH
KV = GROUPS * DH
BW = 2048
BG = 16
NGATE = 3 * HEADS
L_CMP, STRIDE = 32, 16
NC = (T - L_CMP) // STRIDE + 1
BUCKETS, MAX_DIST = 32, 128
WINDOW, L_SEL, N_SEL = 512, 64, 16
EPS = 1e-6
MASKED = -1e30
SCALE = float(DH) ** -0.5
assert T <= WINDOW and T // L_SEL <= N_SEL

C_Q, C_KV, C_GATE = 0, AW, AW + 6 * KV
C_ZA = C_GATE + NGATE
C_U, C_V, C_ZB = C_ZA + AW, C_ZA + AW + BW, C_ZA + AW + 2 * BW
C_MA = C_ZA + AW + 3 * BW
IN_WIDTH = C_MA + 2 * D

NB = 512
KG = 2
GE = KG * NB
RING = 4
AHEAD = 3
SL = KD // KG
YSL = AW // P // KG
GATE_KT = 8
GATE_SL = KD // GATE_KT

H_CMP, H_KV, H_Q, H_U, H_V, H_ZB, H_ZA, H_M, H_Y, H_W = 0, 2, 6, 10, 14, 18, 22, 26, 42, 58
G_GATE = SL * H_U


def granule_of(half):
    if half <= H_Q + 3:
        return SL * half
    if half <= H_Y:
        return SL * half + GATE_SL
    if half <= H_W:
        return granule_of(H_Y) + YSL * (half - H_Y)
    return granule_of(H_W) + SL * (half - H_W)


G_END = granule_of(H_W) + SL * (D // NB)


def buckets():
    n = np.arange(T, dtype=np.int32)
    exact = BUCKETS // 2
    nf = np.maximum(n, 1).astype(np.float32)
    large = exact + (np.log(nf / np.float32(exact)) / np.float32(np.log(MAX_DIST / exact))
                     * np.float32(BUCKETS - exact)).astype(np.int32)
    return np.where(n < exact, n, np.minimum(large, BUCKETS - 1))


def selectors():
    b = buckets()
    falling = np.zeros((BUCKETS + 1, 2 * T), np.float32)
    rising = np.zeros((BUCKETS + 1, 2 * T), np.float32)
    for i in range(2 * T):
        dist = T - 1 - i
        falling[b[dist] if dist >= 0 else BUCKETS, i] = 1.0
        dist = i - T
        rising[b[dist] if dist >= 0 else BUCKETS, i] = 1.0
    return np.concatenate([falling, rising], axis=1)


def wait(eng, sem, value):
    if isinstance(value, int) and value <= 0:
        return
    eng.wait_ge(sem, value)


def layer_kernel(nc, x_nat, x_t, rel_bias, pre_norm_t, w_in, pe_t, w1_k, w2_k, w1_v, w2_v, w_out_a,
                 sgu_norm, sgu_w_t, sgu_b_t, w_out_b, w_out, post_norm, select, any_valid, out):
    m_dram = nc.dram_tensor("merge_gates", (2 * D // NB, P, NT, NB), F32, kind="Internal").ap()
    fall_dram = nc.dram_tensor("bias_falling", (HEADS, 2 * T), F32, kind="Internal")
    bias_dram = nc.dram_tensor("bias_tiles", (HEADS, P, T), F32, kind="Internal").ap()

    with ExitStack() as ctx:
        def sb(name, shape, dt=F32, stack=ctx):
            return stack.enter_context(nc.sbuf_tensor(name, shape, dt))

        def sem(name):
            return ctx.enter_context(nc.semaphore(name))

        raw = sb("raw", [P, RING, GE])
        w_hi = sb("w_hi", [P, RING, GE], F32R)
        w_lo = sb("w_lo", [P, RING, GE], F32R)
        a_hi = sb("a_hi", [P, KD, T], F32R)
        a_lo = sb("a_lo", [P, KD, T], F32R)
        ident = sb("ident", [P, P])
        cmp_bias = sb("cmp_bias", [P, NT, NC, HEADS])
        vc = sb("vc", [NC, KV])
        kc = sb("kc", [P, GROUPS * NC])
        gates = sb("gates", [P, NT, NGATE])
        g_pre = sb("g_pre", [P, KD])
        valid = sb("valid", [P, 1])
        eps = sb("eps", [P, 1])
        sgu_bias = sb("sgu_bias", [P, BG])
        x_ss = sb("x_ss", [P, NT, 4])
        v_ss = sb("v_ss", [P, NT, 4])
        y_ss = sb("y_ss", [P, NT, D // NB])
        mean = sb("mean", [P, NT])
        root = sb("root", [P, NT])
        rstd = sb("rstd", [P, NT])
        v_rstd = sb("v_rstd", [P, NT])
        y_rstd = sb("y_rstd", [P, NT])
        neg_max = sb("neg_max", [P, NT])
        sums = sb("sums", [P, 3, NT])
        recip = sb("recip", [P, NT])
        coef = sb("coef", [P, NT])

        first = ExitStack()
        ztmp = sb("ztmp", [P, NT, NB], stack=first)
        bias = sb("bias", [P, 2, T], stack=first)
        scores = sb("scores", [P, 3 * P], stack=first)
        probs_t = sb("probs_t", [P, 3 * P], stack=first)
        q_now = sb("q_now", [P, T], stack=first)
        v_b = sb("v_b", [P, NT, BW], stack=first)
        k_t = sb("k_t", [P, 2, GROUPS, T], stack=first)
        v_n = sb("v_n", [P, 2, NT, KV], stack=first)
        cmp_t = sb("cmp_t", [P, 2, GROUPS, T], stack=first)
        stage = sb("stage", [P, 2, NT, NB], stack=first)
        u_b = sb("u_b", [P, NT, BW], stack=first)
        q_o = sb("q_o", [P, HEADS, T], stack=first)
        first.close()
        xt_raw = [(u_b if s < 8 else q_o)[:].rearrange("p a b -> p (a b)")[:, (s % 8) * KG * T:(s % 8 + 1) * KG * T]
                  for s in range(SL)]
        x_sq = [v_b[:, j // 2, (j % 2) * 1024:(j % 2 + 1) * 1024] for j in range(4)]
        w1 = [t[:].rearrange("p a b -> p (a b)").rearrange("p (l e) -> p l e", l=L_CMP) for t in (u_b, q_o)]
        late = [v_b[:, i, 0:GROUPS * T] for i in range(2)]
        w2 = [v_b[:, i, GROUPS * T:GROUPS * T + P] for i in range(2)]
        pe = [v_b[:, i, GROUPS * T + P:GROUPS * T + P + L_CMP] for i in range(2)]
        hid = [v_b[:, i, GROUPS * T + 256:GROUPS * T + 256 + GROUPS * NC] for i in range(2)]
        sgu_wt = cmp_t[:].rearrange("p a g t -> p (a g t)").rearrange("p (g t) -> p g t", g=BG)
        sgu_g = stage[:].rearrange("p a b c -> p (a b c)")[:, 0:BW]
        pick = k_t[:].rearrange("p a g t -> p (a g t)")[0:BUCKETS + 1, 0:4 * T]
        rel = k_t[:].rearrange("p a g t -> p (a g t)")[0:BUCKETS + 1, 4 * T:4 * T + HEADS]
        falling = v_n[:].rearrange("p a b c -> p (a b c)")[0:HEADS, 0:2 * T]

        second = ExitStack()
        m_out = sb("m_out", [P, 2, NT, NB], stack=second)
        sb("pad2", [P, 512], stack=second)
        b_hi = sb("b_hi", [P, AW // P, T], F32R, stack=second)
        b_lo = sb("b_lo", [P, AW // P, T], F32R, stack=second)
        o_hi = sb("o_hi", [P, AW // P, T], F32R, stack=second)
        o_lo = sb("o_lo", [P, AW // P, T], F32R, stack=second)
        m_in = sb("m_in", [P, 2, NT, NB], stack=second)
        second.close()
        merged, part_a = m_out[:, 0], m_out[:, 1]

        third = ExitStack()
        junk = sb("junk", [P, NT, NB], stack=third)
        sb("pad3", [P, 2560 - NT * NB], stack=third)
        y = sb("y", [P, NT, D], stack=third)
        x_res = sb("x_res", [P, NT, D], stack=third)
        g_post = sb("g_post", [P, D], stack=third)
        third.close()

        acc = ctx.enter_context(nc.psum_tensor("acc", [P, 2, NT, 512], F32))
        ps_s = ctx.enter_context(nc.psum_tensor("ps_s", [P, 512], F32))
        ps_t = ctx.enter_context(nc.psum_tensor("ps_t", [P, 512], F32))
        ps_o = ctx.enter_context(nc.psum_tensor("ps_o", [P, 512], F32))
        ps_x = ctx.enter_context(nc.psum_tensor("ps_x", [P, 512], F32))

        raw_landed = [sem(f"raw_landed{s}") for s in range(RING)]
        hi_ready, lo_ready = sem("hi_ready"), sem("lo_ready")
        granule_used = sem("granule_used")
        evac_act, evac_dve = sem("evac_act"), sem("evac_dve")
        xt_landed = [sem(f"xt_landed{s}") for s in range(SL)]
        g_landed, ident_made, eps_made = sem("g_landed"), sem("ident_made"), sem("eps_made")
        h_hi, h_lo = sem("h_hi"), sem("h_lo")
        xn_landed = [sem(f"xn_landed{s}") for s in range(4)]
        x_squared, x_mean, x_root, x_rstd = sem("x_squared"), sem("x_mean"), sem("x_root"), sem("x_rstd")
        pick_landed, rel_masked = sem("pick_landed"), sem("rel_masked")
        fall_done, fall_copied, fall_stored, bias_stored = (sem("fall_done"), sem("fall_copied"),
                                                            sem("fall_stored"), sem("bias_stored"))
        cmpb_done, cmpb_copied = sem("cmpb_done"), sem("cmpb_copied")
        turned, turned_copied = sem("turned"), sem("turned_copied")
        cmpw_landed = [sem("cmpw_landed_k"), sem("cmpw_landed_v")]
        pe_added, hid_done, hid_act, cmp_done, cmp_copied = (sem("pe_added"), sem("hid_done"), sem("hid_act"),
                                                            sem("cmp_done"), sem("cmp_copied"))
        gate_act, gate_valid = sem("gate_act"), sem("gate_valid")
        small_landed = sem("small_landed")
        bias_landed = [sem("bias_landed0"), sem("bias_landed1")]
        q_ready, scores_done, biased, maxed, probs_ready = (sem("q_ready"), sem("scores_done"), sem("biased"),
                                                            sem("maxed"), sem("probs_ready"))
        probs_turned, probs_copied, pv_done, coef_steps, o_added = (sem("probs_turned"), sem("probs_copied"),
                                                                    sem("pv_done"), sem("coef_steps"), sem("o_added"))
        sguw_landed, sguw_masked, sgug_landed = sem("sguw_landed"), sem("sguw_masked"), sem("sgug_landed")
        v_squared, v_scaled = sem("v_squared"), sem("v_scaled")
        v_mean, v_root, v_rs, v_normed = sem("v_mean"), sem("v_root"), sem("v_rs"), sem("v_normed")
        mixed, gated = sem("mixed"), sem("gated")
        z_used = sem("z_used")
        o_turned, o_hi_done, o_lo_done = sem("o_turned"), sem("o_hi_done"), sem("o_lo_done")
        m_act, m_stored = sem("m_act"), [sem("m_stored0"), sem("m_stored1")]
        m_loaded = [sem("m_loaded_a"), sem("m_loaded_b")]
        merge_steps = sem("merge_steps")
        m_turned, m_hi_done, m_lo_done = sem("m_turned"), sem("m_hi_done"), sem("m_lo_done")
        y_squared, y_weighted = sem("y_squared"), sem("y_weighted")
        res_landed, gpost_landed = sem("res_landed"), sem("gpost_landed")
        y_mean, y_root, y_rs, out_ready, out_stored = (sem("y_mean"), sem("y_root"), sem("y_rs"), sem("out_ready"),
                                                       sem("out_stored"))

        block = ctx.enter_context(nc.Block())

        @block.sync
        def _(sp):
            def load(g, slot, w, row, col, kt=KG, width=NB):
                pitch = w.shape[1]
                offset = col + row * pitch
                if not isinstance(offset, int):
                    offset = sp.snap(offset)
                wait(sp, lo_ready, g - RING + 1)
                src = bass.AP(w.tensor, offset, [[pitch, P], [P * pitch, kt], [1, width]])
                sp.dma_start(raw[:, slot, 0:kt * width].rearrange("p (a n) -> p a n", a=kt), src
                             ).then_inc(raw_landed[slot], 16)

            def half(g, w, col, n=SL):
                for s in range(n):
                    load(g + s, s % RING, w, s * KG * P, col)

            sp.dma_start(g_pre[:], pre_norm_t).then_inc(g_landed, 16)
            for s in range(SL):
                sp.dma_start(xt_raw[s].rearrange("p (a t) -> p a t", a=KG),
                             x_t[s * KG * P:(s + 1) * KG * P, :].rearrange("(a p) t -> p a t", p=P)
                             ).then_inc(xt_landed[s], 16)
                load(s, s % RING, w_in, s * KG * P, C_KV)
            half(SL, w_in, C_KV + KV)
            with sp.Fori(0, 2) as i:
                for par in range(2):
                    half(granule_of(H_KV + par) + 2 * SL * i, w_in, (C_KV + 2 * KV + par * KV) + 2 * KV * i)
            with sp.Fori(0, 2) as i:
                for par in range(2):
                    half(granule_of(H_Q + par) + 2 * SL * i, w_in, (C_Q + par * NB) + 2 * NB * i)
            for s in range(GATE_SL):
                load(G_GATE + s, s % RING, w_in, s * GATE_KT * P, C_GATE, GATE_KT, NGATE)
            for h0, col in ((H_U, C_U), (H_V, C_V), (H_ZB, C_ZB), (H_ZA, C_ZA)):
                with sp.Fori(0, 2) as i:
                    for par in range(2):
                        half(granule_of(h0 + par) + 2 * SL * i, w_in, (col + par * NB) + 2 * NB * i)
            with sp.Fori(0, D // NB) as i:
                for par in range(2):
                    half(granule_of(H_M + par) + 2 * SL * i, w_in, (C_MA + par * NB) + 2 * NB * i)
            with sp.Fori(0, D // NB) as i:
                for par, w in enumerate((w_out_a, w_out_b)):
                    half(granule_of(H_Y + par) + 2 * YSL * i, w, i * NB, YSL)
            with sp.Fori(0, D // NB // 2) as i:
                for par in range(2):
                    half(granule_of(H_W + par) + 2 * SL * i, w_out, par * NB + 2 * NB * i)
            out_t = out[0].rearrange("(a p) n -> p a n", p=P)
            for k in range(8):
                j, c = k % 2, k // 2
                sp.wait_ge(out_ready, k + 1)
                sp.dma_start(out_t[:, j, c * 1024:(c + 1) * 1024],
                             y[:, j, c * 1024:(c + 1) * 1024]).then_inc(out_stored, 16)
            sp.wait_ge(out_stored, 16 * 8)

        @block.gpsimd
        def _(pool):
            pool.memset(ident[:], 0.0).then_inc(ident_made, 1)
            pool.wait_ge(ident_made, 1)
            pool.affine_select(out=ident[:], in_=ident[:], compare_op=ALU.not_equal, fill=1.0, base=0,
                               pattern=[[-1, P]], channel_multiplier=1).then_inc(ident_made, 1)
            pool.dma_start(pick, select).then_inc(pick_landed, 16)
            pool.dma_start(rel[0:BUCKETS, :], rel_bias).then_inc(pick_landed, 16)
            pool.wait_ge(h_lo, 8)
            for k in range(8):
                j, c = k % 2, k // 2
                if k >= 4:
                    pool.wait_ge(x_squared, k - 3)
                pool.dma_start(x_sq[k % 4], x_nat[j * P:(j + 1) * P, c * 1024:(c + 1) * 1024]
                               ).then_inc(xn_landed[k % 4], 16)
            pool.dma_start(valid[:], any_valid).then_inc(small_landed, 16)
            pool.dma_start(sgu_bias[:], sgu_b_t).then_inc(small_landed, 16)
            pool.wait_ge(fall_copied, 1)
            pool.dma_start(fall_dram.ap(), falling).then_inc(fall_stored, 16)
            pool.wait_ge(fall_stored, 16)
            pool.dma_start(bias_dram, bass.AP(fall_dram, P - 1, [[2 * T, HEADS], [-1, P], [1, T]])
                           ).then_inc(bias_stored, 16)
            pool.wait_ge(h_lo, KD)
            for i, (w1_d, w2_d) in enumerate(((w1_k, w2_k), (w1_v, w2_v))):
                pool.dma_start(w1[i], w1_d.rearrange("(l d) e -> d l e", d=DH)).then_inc(cmpw_landed[i], 16)
                pool.wait_ge(x_squared, 8)
                pool.dma_start(w2[i], w2_d).then_inc(cmpw_landed[i], 16)
                pool.dma_start(pe[i], pe_t[i]).then_inc(cmpw_landed[i], 16)
            pool.wait_ge(hid_done, 2)
            pool.dma_start(sgu_wt, sgu_w_t).then_inc(sguw_landed, 16)
            pool.wait_ge(bias_stored, 16)
            for h in range(2):
                pool.dma_start(bias[:, h, :], bias_dram[h]).then_inc(bias_landed[h], 16)
            pool.wait_ge(sguw_landed, 16)
            pool.affine_select(out=sgu_wt, in_=sgu_wt, compare_op=ALU.is_ge, fill=0.0, base=0,
                               pattern=[[0, BG], [1, P]], channel_multiplier=-1).then_inc(sguw_masked, 1)
            pool.wait_ge(turned, 8)
            pool.dma_start(sgu_g, sgu_norm.partition_broadcast(P)).then_inc(sgug_landed, 16)
            pool.wait_ge(sgug_landed, 16)
            pool.wait_ge(turned_copied, 16)

            def head_half(sec, par, i):
                h = (4 * sec + par) + 2 * i
                half = (H_U + 4 * sec + par) + 2 * i
                cols = ds(par * NB + 2 * NB * i, NB)
                pool.wait_ge(biased, 6 * h + 6)
                if sec < 3 or i == 0:
                    pool.dma_start(bias[:, par, :], bias_dram[ds(h + 2, 1)].rearrange("a p t -> p (a t)")
                                   ).then_inc(bias_landed[par], 16)
                if sec < 3 or i == 0 or par == 0:
                    pool.tensor_copy(q_now[:], q_o[:, ds(h + 1, 1), :].rearrange("p a t -> p (a t)")
                                     ).then_inc(q_ready, 1)
                if sec == 1:
                    pool.wait_ge(v_squared, (2 * par + 2) + 4 * i)
                    for j in range(NT):
                        pool.tensor_tensor(v_b[:, j, cols], v_b[:, j, cols], sgu_g[:, cols], ALU.mult
                                           ).then_inc(v_scaled, 1)
                if sec == 2:
                    pool.wait_ge(evac_act, half + 1)
                    pool.wait_ge(mixed, 2 * BG)
                    for j in range(NT):
                        pool.tensor_tensor(u_b[:, j, cols], u_b[:, j, cols], ztmp[:, j, :], ALU.mult
                                           ).then_inc(z_used, 1)
                if sec == 3:
                    pool.wait_ge(evac_act, half + 1)
                    pool.wait_ge(o_added, 24 * (par + 1) + 48 * i)
                    for j in range(NT):
                        o4 = q_o[:, ds(4 * par + 8 * i, 4), j * DH:(j + 1) * DH]
                        pool.tensor_tensor(o4, o4, ztmp[:, j, :].rearrange("p (h d) -> p h d", h=4), ALU.mult
                                           ).then_inc(z_used, 1)

            pool.tensor_copy(q_now[:], q_o[:, 0, :]).then_inc(q_ready, 1)
            for sec in range(3):
                with pool.Fori(0, 2) as i:
                    for par in range(2):
                        head_half(sec, par, i)
            for i in range(2):
                for par in range(2):
                    head_half(3, par, i)
            with pool.Fori(0, D // NB) as i:
                for par in range(2):
                    pool.wait_ge(m_act, (2 * par + 2) + 4 * i)
                    pool.dma_start(m_dram[ds(par + 2 * i, 1)].rearrange("c p a n -> p (c a) n"), m_out[:, par]
                                   ).then_inc(m_stored[par], 16)
            for par in range(2):
                pool.wait_ge(m_stored[par], 16 * (D // NB))

            def load_gates(c, k):
                pool.dma_start(m_in[:, k], m_dram[ds(k * (D // NB) + c, 1)].rearrange("c p a n -> p (c a) n")
                               ).then_inc(m_loaded[k], 16)

            pool.wait_ge(o_lo_done, 2 * AW // P)
            for k in range(2):
                load_gates(0, k)
            with pool.Fori(0, D // NB - 1) as c:
                pool.wait_ge(merge_steps, 5 * c + 2)
                load_gates(c + 1, 0)
                pool.wait_ge(merge_steps, 5 * c + 4)
                load_gates(c + 1, 1)
            pool.wait_ge(granule_used, granule_of(H_W))
            pool.wait_ge(merge_steps, 5 * (D // NB))
            with pool.Fori(0, D // NB) as c:
                cols = ds(c * NB, NB)
                pool.dma_start(g_post[:, cols], post_norm[cols].partition_broadcast(P)).then_inc(gpost_landed, 16)
                pool.dma_start(x_res[:, :, cols], x_nat[:, cols].rearrange("(a p) n -> p a n", p=P)
                               ).then_inc(res_landed, 16)
                pool.wait_ge(gpost_landed, 16 * c + 16)
                pool.wait_ge(y_squared, 2 * c + 2)
                for j in range(NT):
                    pool.tensor_tensor(y[:, j, cols], y[:, j, cols], g_post[:, cols],
                                       ALU.mult).then_inc(y_weighted, 1)

        @block.scalar
        def _(act):
            def split(g, slot):
                act.wait_ge(raw_landed[slot], 16 + 4 * (g - slot))
                wait(act, granule_used, g - RING + 1)
                act.activation(w_hi[:, slot, :], raw[:, slot, :], ACT.Copy).then_inc(hi_ready, 1)

            def split_h(s):
                act.wait_ge(xt_landed[s], 16)
                for a in range(KG):
                    kt = KG * s + a
                    act.activation(a_hi[:, kt, :], xt_raw[s][:, a * T:(a + 1) * T], ACT.Copy,
                                   scale=g_pre[:, kt:kt + 1]).then_inc(h_hi, 1)

            def half_end(g_end):
                act.wait_ge(granule_used, g_end)

            def to_sbuf(dest, pair, func=ACT.Copy, sem_=None, scale=None):
                for j in range(NT):
                    ins = act.activation(dest(j), acc[:, pair, j, :], func, scale=rstd[:, j:j + 1])
                    if j == NT - 1:
                        ins.then_inc(evac_act, 1)
                    elif sem_ is not None:
                        ins.then_inc(sem_, 1)
                return ins

            def attend(k, h, par):
                for b, slot in enumerate((2, 6, 10)):
                    n = 3 * h + b
                    if k == slot:
                        act.wait_ge(maxed, 2 * n + 2)
                        parts = ((1, scores[:, 0:T]), (0, scores[:, T:T + P])) if b < 2 else \
                            tuple((j, scores[:, 16 * j:16 * j + NC]) for j in range(NT))
                        for j, part in parts:
                            act.activation(part, part, ACT.Exp, bias=neg_max[:, j:j + 1],
                                           accum_out=sums[:, b, j:j + 1]).then_inc(probs_ready, 1)
                    if k == slot + 2:
                        act.wait_ge(probs_turned, n + 1)
                        rows, width = (P, 3 * P) if b < 2 else (NC, T)
                        act.activation(probs_t[0:rows, 0:width], ps_t[0:rows, 0:width], ACT.Copy
                                       ).then_inc(probs_copied, 1)

            act.wait_ge(eps_made, 1)
            act.activation(root[:, 0:1], eps[:], ACT.Copy)
            act.wait_ge(g_landed, 16)
            for s in range(AHEAD):
                split_h(s)
                split(s, s)
            for par in range(2):
                for k in range(SL):
                    if par == 0 and k + AHEAD < SL:
                        split_h(k + AHEAD)
                    split(SL * par + k + AHEAD, (k + AHEAD) % RING)
                if par == 0:
                    act.wait_ge(x_mean, 1)
                    act.wait_ge(eps_made, 1)
                    act.activation(root[:], mean[:], ACT.Sqrt, bias=eps[:, 0:1], scale=1.0 / D).then_inc(x_root, 1)
                    act.wait_ge(x_rstd, 1)
                half_end(SL * (par + 1))
                to_sbuf(lambda j: stage[:, par, j, :], par)
            act.wait_ge(fall_stored, 16)
            with act.Fori(0, 2) as i:
                for par in range(2):
                    g0 = granule_of(H_KV + par) + 2 * SL * i
                    for k in range(SL):
                        split(g0 + k + AHEAD, (k + AHEAD) % RING)
                    half_end(g0 + SL)
                    if par == 0:
                        act.wait_ge(turned, 2 + i)
                        to_sbuf(lambda j: stage[:, 0, j, :], 0)
                    else:
                        to_sbuf(lambda j: v_n[:, ds(i, 1), j, :].rearrange("p a n -> p (a n)"), 1)
            for kv in range(2):
                act.wait_ge(hid_done, kv + 1)
                act.activation(hid[kv], (ps_x if kv == 0 else ps_s)[:, 0:GROUPS * NC], ACT.Silu).then_inc(hid_act, 1)
            with act.Fori(0, 2) as i:
                for par in range(2):
                    g0 = granule_of(H_Q + par) + 2 * SL * i
                    for k in range(SL):
                        split(g0 + k + AHEAD, (k + AHEAD) % RING)
                    half_end(g0 + SL)
                    act.wait_ge(turned, (4 + par) + i)
                    to_sbuf(lambda j: stage[:, par, j, :], par)
            for s in range(GATE_SL):
                split(G_GATE + s + AHEAD, (s + AHEAD) % RING)
            for j, ps in enumerate((ps_x, ps_s)):
                act.wait_ge(granule_used, G_GATE + GATE_SL)
                act.activation(gates[:, j, :], ps[:, 0:NGATE], ACT.Sigmoid, scale=rstd[:, j:j + 1]
                               ).then_inc(gate_act, 1)
            def head_half(sec, par, i, dest, func):
                g0 = granule_of(H_U + 4 * sec + par) + 2 * SL * i
                for k in range(SL):
                    split(g0 + k + AHEAD, (k + AHEAD) % RING)
                    attend(k, (4 * sec + par) + 2 * i, par)
                half_end(g0 + SL)
                if sec >= 2:
                    wait(act, z_used, (8 * (sec - 2) + 2 * par) + 4 * i)
                to_sbuf(dest, par, func)

            for sec, dest in enumerate((u_b, v_b)):
                with act.Fori(0, 2) as i:
                    for par in range(2):
                        cols = ds(par * NB + 2 * NB * i, NB)
                        head_half(sec, par, i, lambda j: dest[:, j, cols], ACT.Gelu_apprx_tanh)
            act.wait_ge(v_mean, 1)
            act.activation(root[:], mean[:], ACT.Sqrt, bias=eps[:, 0:1], scale=1.0 / BW).then_inc(v_root, 1)
            for i in range(2):
                for par in range(2):
                    head_half(2, par, i, lambda j: ztmp[:, j, :], ACT.Silu)
            with act.Fori(0, 2) as i:
                for par in range(2):
                    head_half(3, par, i, lambda j: ztmp[:, j, :], ACT.Silu)

            def merge_gate_half(i, turn):
                for par in range(2):
                    g0 = granule_of(H_M + par) + 2 * SL * i
                    for k in range(SL):
                        split(g0 + k + AHEAD, (k + AHEAD) % RING)
                        if turn is not None and k > 0:
                            turn(SL * par + k - 1)
                    half_end(g0 + SL)
                    if turn is not None:
                        turn(SL * par + SL - 1)
                        act.wait_ge(z_used, 16)
                    else:
                        act.wait_ge(m_stored[par], 16 * i)
                    for j in range(NT):
                        ins = act.activation(m_out[:, par, j, :], acc[:, par, j, :], ACT.Sigmoid,
                                             scale=rstd[:, j:j + 1])
                        ins.then_inc(m_act, 1)

            def turn_hi(q):
                act.wait_ge(o_turned, q + 1)
                dest = (b_hi if q < 16 else o_hi)[:, q % 16, :]
                act.activation(dest, (ps_s if q % 2 == 0 else ps_t)[:, 0:T], ACT.Copy).then_inc(o_hi_done, 1)

            merge_gate_half(0, turn_hi)
            with act.Fori(1, D // NB) as i:
                merge_gate_half(i, None)

            def merged_hi(c, q):
                act.wait_ge(m_turned, 4 * c + q + 1)
                act.activation(a_hi[:, ds(4 * c + q, 1), :].rearrange("p a t -> p (a t)"),
                               (ps_s if q % 2 == 0 else ps_t)[:, 0:T], ACT.Copy).then_inc(m_hi_done, 1)

            def y_half(c, first_):
                g0 = granule_of(H_Y) + 2 * YSL * c
                for k in range(2 * YSL):
                    split(g0 + k + AHEAD, (k + AHEAD) % RING)
                    if not first_ and 2 <= k < 6:
                        merged_hi(c - 1, k - 2)

            y_half(0, True)
            with act.Fori(1, D // NB) as c:
                y_half(c, False)

            def w_half(c, par, n=SL, last_merged=False):
                g0 = granule_of(H_W) + SL * c
                for k in range(n):
                    split(g0 + k + AHEAD, (k + AHEAD) % RING)
                    if last_merged and 2 <= k < 6:
                        merged_hi(D // NB - 1, k - 2)
                half_end(g0 + SL)
                if last_merged:
                    act.wait_ge(merge_steps, 5 * (D // NB))
                for j in range(NT):
                    act.activation(y[:, j, ds(c * NB, NB)], acc[:, par, j, :], ACT.Copy)
                    wait(act, y_squared, 2 * c + (j - 1))
                    act.activation(junk[:, j, :], acc[:, par, j, :], ACT.Square,
                                   accum_out=y_ss[:, j, ds(c, 1)]).then_inc(y_squared, 1)

            w_half(0, 0, last_merged=True)
            w_half(1, 1)
            with act.Fori(1, D // NB // 2 - 1) as i:
                for par in range(2):
                    w_half(2 * i + par, par)
            w_half(D // NB - 2, 0)
            w_half(D // NB - 1, 1, n=SL - AHEAD)
            act.wait_ge(y_mean, 1)
            act.activation(root[:], mean[:], ACT.Sqrt, bias=eps[:, 0:1], scale=1.0 / D).then_inc(y_root, 1)

        @block.vector
        def _(dve):
            def split(g, slot):
                dve.wait_ge(hi_ready, g + 1)
                dve.tensor_tensor(w_lo[:, slot, :], raw[:, slot, :], w_hi[:, slot, :].bitcast(F32), ALU.subtract
                                  ).then_inc(lo_ready, 1)

            def split_h(s):
                for a in range(KG):
                    kt = KG * s + a
                    dve.wait_ge(h_hi, kt + 1)
                    dve.scalar_tensor_tensor(out=a_lo[:, kt, :], in0=xt_raw[s][:, a * T:(a + 1) * T],
                                             scalar=g_pre[:, kt:kt + 1], in1=a_hi[:, kt, :].bitcast(F32),
                                             op0=ALU.mult, op1=ALU.subtract).then_inc(h_lo, 1)

            def square_x(k):
                dve.wait_ge(xn_landed[k % 4], 16 * (k // 4 + 1))
                dve.tensor_tensor_reduce(x_sq[k % 4], x_sq[k % 4], x_sq[k % 4], 1.0, 0.0, ALU.mult, ALU.add,
                                         x_ss[:, k % 2, k // 2:k // 2 + 1]).then_inc(x_squared, 1)

            def turned_to(dest, m):
                dve.wait_ge(turned, m + 1)
                for a, ps in enumerate((ps_t, ps_o)):
                    dve.tensor_copy(dest[:, 2 * a:2 * a + 2, :].rearrange("p g t -> p (g t)"), ps[:]
                                    ).then_inc(turned_copied, 1)

            def attend(k, h, par, sec, i):
                for b, slot in enumerate((1, 5, 9)):
                    n = 3 * h + b
                    if k == slot:
                        if b == 0:
                            dve.wait_ge(bias_landed[par], (32 * sec + 16) + 16 * i)
                        dve.wait_ge(scores_done, n + 1)
                        if not (sec == 0 and par == 0 and b == 0):
                            dve.wait_ge(probs_turned, n)
                        if b < 2:
                            dve.scalar_tensor_tensor(out=scores[:, 0:T], in0=ps_s[:, 0:T], scalar=SCALE,
                                                     in1=bias[:, par, :], op0=ALU.mult, op1=ALU.add
                                                     ).then_inc(biased, 1)
                            dve.scalar_tensor_tensor(out=scores[:, T:T + P], in0=ps_s[:, T:T + P], scalar=SCALE,
                                                     in1=bias[:, par, P:T], op0=ALU.mult, op1=ALU.add
                                                     ).then_inc(biased, 1)
                            dve.wait_ge(biased, 2 * n + 2)
                            dve.tensor_reduce(neg_max[:, 1:2], scores[:, 0:T], AX.X, ALU.max, negate=True
                                              ).then_inc(maxed, 1)
                            dve.tensor_reduce(neg_max[:, 0:1], scores[:, T:T + P], AX.X, ALU.max, negate=True
                                              ).then_inc(maxed, 1)
                        else:
                            both = scores[:, 0:32].rearrange("p (j n) -> p j n", j=NT)[:, :, 0:NC]
                            dve.scalar_tensor_tensor(
                                out=both, in0=ps_s[:, 0:32].rearrange("p (j n) -> p j n", j=NT)[:, :, 0:NC],
                                scalar=SCALE, in1=cmp_bias[:, :, :, ds(h, 1)].rearrange("p j n a -> p j (n a)"),
                                op0=ALU.mult, op1=ALU.add).then_inc(biased, 2)
                            dve.wait_ge(biased, 2 * n + 2)
                            dve.tensor_reduce(neg_max[:], both, AX.X, ALU.max, negate=True).then_inc(maxed, 2)
                    if k == slot + 5:
                        dve.wait_ge(probs_ready, 2 * n + 2)
                        dve.reciprocal(recip[:], sums[:, b, :]).then_inc(coef_steps, 1)
                        dve.wait_ge(coef_steps, 2 * n + 1)
                        dve.tensor_tensor(coef[:], recip[:],
                                          gates[:, :, ds(3 * h + GATE[b], 1)].rearrange("p j a -> p (j a)"), ALU.mult
                                          ).then_inc(coef_steps, 1)
                        dve.wait_ge(coef_steps, 2 * n + 2)
                        dve.wait_ge(pv_done, n + 1)
                        for j in range(NT):
                            o_h = q_o[:, ds(h, 1), j * DH:(j + 1) * DH].rearrange("p a d -> p (a d)")
                            if b == 0:
                                dve.tensor_scalar(o_h, ps_o[:, j * DH:(j + 1) * DH], coef[:, j:j + 1], None, ALU.mult
                                                  ).then_inc(o_added, 1)
                            else:
                                dve.wait_ge(o_added, 2 * n)
                                dve.scalar_tensor_tensor(out=o_h, in0=ps_o[:, j * DH:(j + 1) * DH],
                                                         scalar=coef[:, j:j + 1], in1=o_h, op0=ALU.mult,
                                                         op1=ALU.add).then_inc(o_added, 1)

            def mix(m):
                dve.wait_ge(gated, m + 1)
                for q in range(4):
                    grp, j = 2 * m + q // 2, q % 2
                    cols = slice(grp * P, (grp + 1) * P)
                    dve.scalar_tensor_tensor(out=u_b[:, j, cols], in0=ps_x[:, q * P:(q + 1) * P],
                                             scalar=sgu_bias[:, grp:grp + 1], in1=u_b[:, j, cols],
                                             op0=ALU.add, op1=ALU.mult).then_inc(mixed, 1)

            dve.memset(eps[:], EPS).then_inc(eps_made, 1)
            dve.memset(rel[BUCKETS:BUCKETS + 1, :], MASKED).then_inc(rel_masked, 1)
            for s in range(AHEAD):
                split_h(s)
                split(s, s)
            for par in range(2):
                for k in range(SL):
                    if par == 0 and k + AHEAD < SL:
                        split_h(k + AHEAD)
                    split(SL * par + k + AHEAD, (k + AHEAD) % RING)
                    if par == 0 and k == 3:
                        dve.wait_ge(fall_done, 1)
                        dve.tensor_copy(falling, ps_s[0:HEADS, :]).then_inc(fall_copied, 1)
                        dve.wait_ge(cmpb_done, 1)
                        dve.tensor_copy(cmp_bias[:].rearrange("p j n h -> p (j n h)"), ps_x[:, 0:NT * NC * HEADS]
                                        ).then_inc(cmpb_copied, 1)
                    if par == 0 and k >= 12:
                        square_x(2 * (k - 12))
                        square_x(2 * (k - 12) + 1)
                    if par == 1 and k == 2:
                        turned_to(cmp_t[:, 0], 0)
                if par == 0:
                    dve.wait_ge(x_squared, 8)
                    dve.tensor_reduce(mean[:], x_ss[:], AX.X, ALU.add).then_inc(x_mean, 1)
                    dve.wait_ge(x_root, 1)
                    dve.reciprocal(rstd[:], root[:]).then_inc(x_rstd, 1)
            turned_to(cmp_t[:, 1], 1)
            dve.wait_ge(turned_copied, 4)
            for kv in range(2):
                dve.wait_ge(cmpw_landed[kv], 48)
                kvt = cmp_t[:, kv].rearrange("p g (j r) -> p (g j) r", r=STRIDE)
                for src, half_ in ((late[kv].rearrange("p (j r) -> p j r", r=STRIDE), 1), (kvt, 0)):
                    emb = pe[kv][:, half_ * STRIDE:(half_ + 1) * STRIDE].rearrange("p (a r) -> p a r", a=1)
                    emb = emb.broadcast_to([P, GROUPS * T // STRIDE, STRIDE])
                    dve.tensor_tensor(src, kvt, emb, ALU.add).then_inc(pe_added, 1)
            with dve.Fori(0, 2) as i:
                for par in range(2):
                    g0 = granule_of(H_KV + par) + 2 * SL * i
                    for k in range(SL):
                        split(g0 + k + AHEAD, (k + AHEAD) % RING)
                        if par == 1 and k == 2:
                            turned_to(k_t[:, ds(i, 1)].rearrange("p a g t -> p (a g) t"), 2 + i)
            dve.wait_ge(cmp_done, 1)
            dve.tensor_copy(kc[:], ps_t[:, 0:GROUPS * NC]).then_inc(cmp_copied, 1)
            dve.wait_ge(cmp_done, 2)
            dve.tensor_copy(vc[:], ps_o[0:NC, :]).then_inc(cmp_copied, 1)
            with dve.Fori(0, 2) as i:
                for par in range(2):
                    g0 = granule_of(H_Q + par) + 2 * SL * i
                    for k in range(SL):
                        split(g0 + k + AHEAD, (k + AHEAD) % RING)
                        if par == 1 and k == 2:
                            turned_to(q_o[:, ds(8 * i, 4), :], 4 + 2 * i)
                turned_to(q_o[:, ds(8 * i + 4, 4), :], 5 + 2 * i)
            for s in range(GATE_SL):
                split(G_GATE + s + AHEAD, (s + AHEAD) % RING)
            dve.wait_ge(gate_act, 2)
            dve.wait_ge(small_landed, 32)
            own = gates[:, 0, :].rearrange("p (h b) -> p h b", b=3)[:, :, 0]
            dve.tensor_scalar(own, own, valid[:, 0:1], None, ALU.mult).then_inc(gate_valid, 1)
            dve.wait_ge(gate_valid, 1)
            with dve.Fori(0, 2) as i:
                for par in range(2):
                    g0 = granule_of(H_U + par) + 2 * SL * i
                    for k in range(SL):
                        split(g0 + k + AHEAD, (k + AHEAD) % RING)
                        attend(k, par + 2 * i, par, 0, i)
            for half in range(4):
                for k in range(SL):
                    split(granule_of(H_V + half) + k + AHEAD, (k + AHEAD) % RING)
                    attend(k, 4 + half, half % 2, 1, half // 2)
                dve.wait_ge(evac_act, H_V + half + 1)
                for j in range(NT):
                    v_half = v_b[:, j, half * NB:(half + 1) * NB]
                    dve.tensor_tensor_reduce(ztmp[:, j, :], v_half, v_half, 1.0, 0.0, ALU.mult, ALU.add,
                                             v_ss[:, j, half:half + 1]).then_inc(v_squared, 1)
            dve.wait_ge(v_squared, 8)
            dve.tensor_reduce(mean[:], v_ss[:], AX.X, ALU.add).then_inc(v_mean, 1)
            dve.wait_ge(v_root, 1)
            dve.reciprocal(v_rstd[:], root[:]).then_inc(v_rs, 1)
            dve.wait_ge(v_rs, 1)
            dve.wait_ge(v_scaled, 8)
            for j in range(NT):
                dve.tensor_scalar(v_b[:, j, :], v_b[:, j, :], v_rstd[:, j:j + 1], None, ALU.mult
                                  ).then_inc(v_normed, 1)
            for half in range(4):
                sec, par = 2, half % 2
                g0 = granule_of(H_ZB + half)
                for k in range(SL):
                    split(g0 + k + AHEAD, (k + AHEAD) % RING)
                    attend(k, 8 + half, par, sec, half // 2)
                    if half == 0 and 2 <= k < 2 + BG // 2:
                        mix(k - 2)
            with dve.Fori(0, 2) as i:
                for par in range(2):
                    g0 = granule_of(H_ZA + par) + 2 * SL * i
                    for k in range(SL):
                        split(g0 + k + AHEAD, (k + AHEAD) % RING)
                        attend(k, (12 + par) + 2 * i, par, 3, i)

            def turn_lo(q):
                dve.wait_ge(o_hi_done, q + 1)
                hi, lo = (b_hi, b_lo) if q < 16 else (o_hi, o_lo)
                dve.tensor_tensor(lo[:, q % 16, :], (ps_s if q % 2 == 0 else ps_t)[:, 0:T],
                                  hi[:, q % 16, :].bitcast(F32), ALU.subtract).then_inc(o_lo_done, 1)

            for par in range(2):
                g0 = granule_of(H_M + par)
                for k in range(SL):
                    split(g0 + k + AHEAD, (k + AHEAD) % RING)
                    if k > 0:
                        turn_lo(SL * par + k - 1)
                turn_lo(SL * par + SL - 1)
            with dve.Fori(1, D // NB) as i:
                for par in range(2):
                    g0 = granule_of(H_M + par) + 2 * SL * i
                    for k in range(SL):
                        split(g0 + k + AHEAD, (k + AHEAD) % RING)

            def merged_lo(c, q):
                dve.wait_ge(m_hi_done, 4 * c + q + 1)
                kt = ds(4 * c + q, 1)
                dve.tensor_tensor(a_lo[:, kt, :].rearrange("p a t -> p (a t)"), (ps_s if q % 2 == 0 else ps_t)[:, 0:T],
                                  a_hi[:, kt, :].rearrange("p a t -> p (a t)").bitcast(F32), ALU.subtract
                                  ).then_inc(m_lo_done, 1)

            def y_half(c, first_):
                g0 = granule_of(H_Y) + 2 * YSL * c
                for k in range(2 * YSL):
                    split(g0 + k + AHEAD, (k + AHEAD) % RING)
                    if not first_ and 2 <= k < 6:
                        merged_lo(c - 1, k - 2)
                    if k == YSL:
                        dve.wait_ge(m_loaded[0], 16 * c + 16)
                        dve.wait_ge(granule_used, g0 + YSL)
                        for j in range(NT):
                            dve.tensor_tensor(part_a[:, j, :], acc[:, 0, j, :], m_in[:, 0, j, :], ALU.mult
                                              ).then_inc(merge_steps, 1)
                dve.wait_ge(m_loaded[1], 16 * c + 16)
                dve.wait_ge(granule_used, g0 + 2 * YSL)
                if not first_:
                    dve.wait_ge(m_turned, 4 * c)
                for j in range(NT):
                    dve.tensor_tensor(merged[:, j, :], acc[:, 1, j, :], m_in[:, 1, j, :], ALU.mult
                                      ).then_inc(merge_steps, 1)
                dve.wait_ge(merge_steps, 5 * c + 4)
                dve.tensor_tensor(merged, merged, part_a, ALU.add).then_inc(merge_steps, 1)

            y_half(0, True)
            with dve.Fori(1, D // NB) as c:
                y_half(c, False)

            g0 = granule_of(H_W)
            for k in range(SL):
                split(g0 + k + AHEAD, (k + AHEAD) % RING)
                if 2 <= k < 6:
                    merged_lo(D // NB - 1, k - 2)
            with dve.Fori(1, D // NB - 1) as c:
                for k in range(SL):
                    split(g0 + SL * c + k + AHEAD, (k + AHEAD) % RING)
            for k in range(SL - AHEAD):
                split(g0 + SL * (D // NB - 1) + k + AHEAD, (k + AHEAD) % RING)
            dve.wait_ge(y_squared, 2 * (D // NB))
            dve.tensor_reduce(mean[:], y_ss[:], AX.X, ALU.add).then_inc(y_mean, 1)
            dve.wait_ge(y_root, 1)
            dve.reciprocal(y_rstd[:], root[:]).then_inc(y_rs, 1)
            dve.wait_ge(y_rs, 1)
            dve.wait_ge(res_landed, 16 * (D // NB))
            for k in range(8):
                j, c = k % 2, k // 2
                dve.wait_ge(y_weighted, 4 * c + 4)
                cols = slice(c * 1024, (c + 1) * 1024)
                dve.scalar_tensor_tensor(out=y[:, j, cols], in0=y[:, j, cols], scalar=y_rstd[:, j:j + 1],
                                         in1=x_res[:, j, cols], op0=ALU.mult, op1=ALU.add).then_inc(out_ready, 1)

        @block.tensor
        def _(pe_):
            def granule(g, slot, pair, s, n, hi, lo):
                pe_.wait_ge(lo_ready, g + 1)
                for a in range(KG):
                    kt = KG * s + a
                    wh, wl = (w[:, slot, a * NB:(a + 1) * NB] for w in (w_hi, w_lo))
                    for j in range(NT):
                        tok = slice(j * P, (j + 1) * P)
                        dst = acc[:, pair, j, :]
                        pe_.matmul(dst, hi[:, kt, tok], wh, start=(kt == 0), stop=False)
                        pe_.matmul(dst, hi[:, kt, tok], wl, start=False, stop=False)
                        last = pe_.matmul(dst, lo[:, kt, tok], wh, start=False, stop=(kt == KG * n - 1))
                last.then_inc(granule_used, 1)

            def transposes(par):
                for grp in range(GROUPS):
                    for j in range(NT):
                        ps = (ps_t, ps_o)[grp // 2]
                        col = (grp % 2) * T + j * P
                        last = pe_.transpose(ps[:, col:col + P], stage[:, par, j, grp * P:(grp + 1) * P], ident[:])
                last.then_inc(turned, 1)

            def attend(k, h, sec, par):
                tiles = ((slice(0, T), slice(P, T), slice(0, T)), (slice(T, T + P), slice(0, P), slice(0, P)))
                for b, slot in enumerate((0, 4, 8)):
                    n = 3 * h + b
                    first_ = sec == 0 and par == 0 and b == 0
                    if k == slot:
                        if b == 0:
                            pe_.wait_ge(q_ready, h + 1)
                        if not first_:
                            pe_.wait_ge(biased, 2 * n)
                        if b < 2:
                            for dst, tok, keys in tiles:
                                last = pe_.matmul(ps_s[:, dst], q_now[:, tok], k_t[:, b, sec, keys],
                                                  start=True, stop=True)
                        else:
                            for j in range(NT):
                                last = pe_.matmul(ps_s[:, 16 * j:16 * j + NC], q_now[:, j * P:(j + 1) * P],
                                                  kc[:, sec * NC:(sec + 1) * NC], start=True, stop=True)
                        last.then_inc(scores_done, 1)
                    if k == slot + 3:
                        pe_.wait_ge(probs_ready, 2 * n + 2)
                        if not first_:
                            pe_.wait_ge(probs_copied, n)
                        if b < 2:
                            for c in range(3):
                                last = pe_.transpose(ps_t[:, c * P:(c + 1) * P], scores[:, c * P:(c + 1) * P],
                                                     ident[:])
                        else:
                            for j in range(NT):
                                last = pe_.transpose(ps_t[0:NC, j * P:(j + 1) * P], scores[:, 16 * j:16 * j + NC],
                                                     ident[:])
                        last.then_inc(probs_turned, 1)
                    if k == slot + 5:
                        pe_.wait_ge(probs_copied, n + 1)
                        if not first_:
                            pe_.wait_ge(o_added, 2 * n)
                        if b < 2:
                            v = v_n[:, b, :, sec * DH:(sec + 1) * DH]
                            pe_.matmul(ps_o[:, 0:DH], probs_t[:, T:T + P], v[:, 0, :], start=True, stop=True)
                            pe_.matmul(ps_o[:, DH:2 * DH], probs_t[:, 0:P], v[:, 0, :], start=True, stop=False)
                            last = pe_.matmul(ps_o[:, DH:2 * DH], probs_t[:, P:T], v[:, 1, :], start=False,
                                              stop=True)
                        else:
                            for j in range(NT):
                                last = pe_.matmul(ps_o[:, j * DH:(j + 1) * DH], probs_t[0:NC, j * P:(j + 1) * P],
                                                  vc[:, sec * DH:(sec + 1) * DH], start=True, stop=True)
                        last.then_inc(pv_done, 1)

            for par in range(2):
                for s in range(SL):
                    if par == 0:
                        pe_.wait_ge(h_lo, KG * (s + 1))
                    granule(SL * par + s, s % RING, par, s, SL, a_hi, a_lo)
                    if par == 0 and s == 1:
                        pe_.wait_ge(rel_masked, 1)
                        pe_.wait_ge(pick_landed, 32)
                        pe_.matmul(ps_s[0:HEADS, :], rel, pick[:, 0:2 * T], start=True, stop=True
                                   ).then_inc(fall_done, 1)
                        for j in range(NT):
                            for n in range(NC):
                                off = 2 * T + T + j * P - STRIDE * n - (L_CMP - 1)
                                col = (j * NC + n) * HEADS
                                last = pe_.matmul(ps_x[:, col:col + HEADS], pick[:, off:off + P], rel,
                                                  start=True, stop=True)
                        last.then_inc(cmpb_done, 1)
                    if par == 1 and s == 1:
                        pe_.wait_ge(evac_act, 1)
                        pe_.wait_ge(ident_made, 2)
                        transposes(0)
            pe_.wait_ge(evac_act, 2)
            pe_.wait_ge(turned_copied, 2)
            transposes(1)
            with pe_.Fori(0, 2) as i:
                for par in range(2):
                    pe_.wait_ge(evac_act, (H_KV + par - 1) + 2 * i)
                    for s in range(SL):
                        granule((granule_of(H_KV + par) + s) + 2 * SL * i, s % RING, par, s, SL, a_hi, a_lo)
                        if par == 1 and s == 1:
                            pe_.wait_ge(evac_act, (H_KV + 1) + 2 * i)
                            pe_.wait_ge(turned_copied, 4 + 2 * i)
                            transposes(0)
            for kv, ps in enumerate((ps_x, ps_s)):
                pe_.wait_ge(cmpw_landed[kv], 48)
                pe_.wait_ge(pe_added, 2 * kv + 2)
                pe_.wait_ge((fall_copied, cmpb_copied)[1 - kv], 1)
                for l in range(L_CMP):
                    src = cmp_t[:, kv].rearrange("p g t -> p (g t)") if l < STRIDE else late[kv]
                    src = src.rearrange("p (g j r) -> p g j r", g=GROUPS, r=STRIDE)
                    j0 = l // STRIDE
                    last = pe_.matmul(ps[:, 0:GROUPS * NC], w1[kv][:, l, :], src[:, :, j0:j0 + NC, l % STRIDE],
                                      start=(l == 0), stop=(l == L_CMP - 1))
                last.then_inc(hid_done, 1)
            pe_.wait_ge(turned_copied, 8)
            pe_.wait_ge(hid_act, 1)
            pe_.matmul(ps_t[:, 0:GROUPS * NC], w2[0], hid[0], start=True, stop=True).then_inc(cmp_done, 1)
            pe_.wait_ge(hid_act, 2)
            for grp in range(GROUPS):
                last = pe_.matmul(ps_o[0:NC, grp * DH:(grp + 1) * DH], hid[1][:, grp * NC:(grp + 1) * NC], w2[1],
                                  start=True, stop=True)
            last.then_inc(cmp_done, 1)
            pe_.wait_ge(cmp_copied, 2)
            with pe_.Fori(0, 2) as i:
                for par in range(2):
                    pe_.wait_ge(evac_act, (H_Q + par - 1) + 2 * i)
                    for s in range(SL):
                        granule((granule_of(H_Q + par) + s) + 2 * SL * i, s % RING, par, s, SL, a_hi, a_lo)
                        if par == 1 and s == 1:
                            pe_.wait_ge(evac_act, (H_Q + 1) + 2 * i)
                            pe_.wait_ge(turned_copied, 8 + 4 * i)
                            transposes(0)
                pe_.wait_ge(evac_act, (H_Q + 2) + 2 * i)
                pe_.wait_ge(turned_copied, 10 + 4 * i)
                transposes(1)
            pe_.wait_ge(hid_act, 2)
            for s in range(GATE_SL):
                pe_.wait_ge(lo_ready, G_GATE + s + 1)
                for a in range(GATE_KT):
                    kt = GATE_KT * s + a
                    wh, wl = (w[:, s % RING, a * NGATE:(a + 1) * NGATE] for w in (w_hi, w_lo))
                    for j, ps in enumerate((ps_x, ps_s)):
                        tok = slice(j * P, (j + 1) * P)
                        pe_.matmul(ps[:, 0:NGATE], a_hi[:, kt, tok], wh, start=(kt == 0), stop=False)
                        pe_.matmul(ps[:, 0:NGATE], a_hi[:, kt, tok], wl, start=False, stop=False)
                        last = pe_.matmul(ps[:, 0:NGATE], a_lo[:, kt, tok], wh, start=False, stop=(kt == KD - 1))
                last.then_inc(granule_used, 1)
            pe_.wait_ge(turned_copied, 16)
            pe_.wait_ge(gate_act, 2)
            for sec, h0 in enumerate((H_U, H_V)):
                with pe_.Fori(0, 2) as i:
                    for par in range(2):
                        pe_.wait_ge(evac_act, (h0 + par - 1) + 2 * i)
                        for s in range(SL):
                            granule((granule_of(h0 + par) + s) + 2 * SL * i, s % RING, par, s, SL, a_hi, a_lo)
                            attend(s, (4 * sec + par) + 2 * i, sec, par)
            for half in range(4):
                pe_.wait_ge(evac_act, H_ZB + half - 1)
                for s in range(SL):
                    granule(granule_of(H_ZB + half) + s, s % RING, half % 2, s, SL, a_hi, a_lo)
                    attend(s, 8 + half, 2, half % 2)
                    if half == 0 and 1 <= s < 1 + BG // 2:
                        m = s - 1
                        if m == 0:
                            pe_.wait_ge(v_normed, 2)
                            pe_.wait_ge(sguw_masked, 1)
                        else:
                            pe_.wait_ge(mixed, 4 * m)
                        for q in range(4):
                            grp, j = 2 * m + q // 2, q % 2
                            last = pe_.matmul(ps_x[:, q * P:(q + 1) * P], sgu_wt[:, grp, :],
                                              v_b[:, j, grp * P:(grp + 1) * P], start=True, stop=True)
                        last.then_inc(gated, 1)
            with pe_.Fori(0, 2) as i:
                for par in range(2):
                    pe_.wait_ge(evac_act, (H_ZA + par - 1) + 2 * i)
                    for s in range(SL):
                        granule((granule_of(H_ZA + par) + s) + 2 * SL * i, s % RING, par, s, SL, a_hi, a_lo)
                        attend(s, (12 + par) + 2 * i, 3, par)

            for par in range(2):
                pe_.wait_ge(evac_act, H_M + par - 1)
                for s in range(SL):
                    granule(granule_of(H_M + par) + s, s % RING, par, s, SL, a_hi, a_lo)
                    q = SL * par + s
                    if q == 0:
                        pe_.wait_ge(z_used, 8)
                    if q == 16:
                        pe_.wait_ge(z_used, 16)
                    wait(pe_, o_lo_done, q - 1)
                    ps = ps_s if q % 2 == 0 else ps_t
                    for j in range(NT):
                        src = u_b[:, j, s * P:(s + 1) * P] if par == 0 else q_o[:, s, j * DH:(j + 1) * DH]
                        last = pe_.transpose(ps[:, j * P:(j + 1) * P], src, ident[:])
                    last.then_inc(o_turned, 1)
            with pe_.Fori(1, D // NB) as i:
                for par in range(2):
                    pe_.wait_ge(m_act, 4 * i - 2 + 2 * par)
                    for s in range(SL):
                        granule((granule_of(H_M + par) + s) + 2 * SL * i, s % RING, par, s, SL, a_hi, a_lo)

            def turn_merged(c, q):
                pe_.wait_ge(merge_steps, 5 * c + 5)
                if q >= 2:
                    pe_.wait_ge(m_lo_done, 4 * c + q - 1)
                ps = ps_s if q % 2 == 0 else ps_t
                for j in range(NT):
                    last = pe_.transpose(ps[:, j * P:(j + 1) * P], merged[:, j, q * P:(q + 1) * P], ident[:])
                last.then_inc(m_turned, 1)

            def y_half(c, first_):
                for k, (hi, lo) in enumerate(((o_hi, o_lo), (b_hi, b_lo))):
                    if first_:
                        pe_.wait_ge(m_act, 4 * (D // NB) - 2 + 2 * k)
                    else:
                        pe_.wait_ge(merge_steps, 5 * c - 3 + 2 * k)
                    for s in range(YSL):
                        granule((granule_of(H_Y) + YSL * k + s) + 2 * YSL * c, s % RING, k, s, YSL, hi, lo)
                        if not first_ and k == 0 and 1 <= s < 5:
                            turn_merged(c - 1, s - 1)

            pe_.wait_ge(o_lo_done, 2 * AW // P)
            y_half(0, True)
            with pe_.Fori(1, D // NB) as c:
                y_half(c, False)

            def w_half(c, par, first_=False):
                if first_:
                    pe_.wait_ge(merge_steps, 5 * (D // NB) - 3)
                for s in range(SL):
                    if first_ and s == SL - 2:
                        pe_.wait_ge(m_lo_done, KD)
                    if first_ and s == 0:
                        pe_.wait_ge(m_lo_done, KD - 4)
                    granule((granule_of(H_W) + s) + SL * c, s % RING, par, s, SL, a_hi, a_lo)
                    if first_ and 1 <= s < 5:
                        turn_merged(D // NB - 1, s - 1)

            w_half(0, 0, True)
            pe_.wait_ge(merge_steps, 5 * (D // NB) - 1)
            w_half(1, 1)
            with pe_.Fori(1, D // NB // 2) as i:
                for par in range(2):
                    pe_.wait_ge(y_squared, 4 * i - 2 + 2 * par)
                    w_half(2 * i + par, par)


GATE = (1, 2, 0)

_OUT = ((1, T, D), "float32")


def kernel(**inputs):
    import concourse.bacc as bacc
    from concourse.bass_utils import run_bass_kernel_spmd

    a = {k: np.asarray(v) for k, v in inputs.items()}
    arrays = {
        "x_nat": a["x"][0],
        "x_t": np.ascontiguousarray(a["x"][0].T),
        "rel_bias": a["rel_bias"],
        "pre_norm_t": np.ascontiguousarray(a["pre_norm"][0].reshape(KD, P).T),
        "w_in": a["w_in"][0],
        "pe_t": np.ascontiguousarray(np.stack([a["cmp_pe_k"][0].T, a["cmp_pe_v"][0].T])),
        "w1_k": a["cmp_w1_k"][0], "w2_k": a["cmp_w2_k"][0],
        "w1_v": a["cmp_w1_v"][0], "w2_v": a["cmp_w2_v"][0],
        "w_out_a": a["w_out_a"][0],
        "sgu_norm": a["sgu_norm"][0],
        "sgu_w_t": np.ascontiguousarray(a["sgu_w"][0].transpose(2, 0, 1)),
        "sgu_b_t": np.ascontiguousarray(a["sgu_b"][0].T),
        "w_out_b": a["w_out_b"][0],
        "w_out": a["w_out"][0],
        "post_norm": a["post_norm"][0],
        "select": selectors(),
        "any_valid": (np.arange(P) >= L_CMP - 1).astype(np.float32).reshape(P, 1),
    }
    nc = bacc.Bacc("TRN2", target_bir_lowering=False, num_devices=1)
    args = [nc.dram_tensor(f"in_{n}", v.shape, mybir.dt.from_np(v.dtype), kind="ExternalInput").ap()
            for n, v in arrays.items()]
    args.append(nc.dram_tensor("out_dram", _OUT[0], F32, kind="ExternalOutput").ap())
    layer_kernel(nc, *args)
    feeds = {f"in_{n}": np.ascontiguousarray(v) for n, v in arrays.items()}
    return run_bass_kernel_spmd(nc, [feeds], core_ids=[0]).results[0]["out_dram"]
```

```python
from contextlib import ExitStack

import numpy as np
import concourse.bass as bass
from concourse import mybir

F32 = mybir.dt.float32
F32R = mybir.dt.float32r
ALU = mybir.AluOpType
ACT = mybir.ActivationFunctionType
AX = mybir.AxisListType
ds = bass.ds

P = 128
T = 256
NT = T // P
D = 4096
KD = D // P
HEADS, GROUPS, DH = 16, 4, 128
AW = HEADS * DH
KV = GROUPS * DH
BW = 2048
BG = 16
NGATE = 3 * HEADS
L_CMP, STRIDE = 32, 16
NC = (T - L_CMP) // STRIDE + 1
BUCKETS, MAX_DIST = 32, 128
WINDOW, L_SEL, N_SEL = 512, 64, 16
EPS = 1e-6
MASKED = -1e30
SCALE = float(DH) ** -0.5
S_LATE = (slice(0, T), slice(NC, NC + T))
S_EARLY = (slice(T, T + P), slice(2 * NC + T, 2 * NC + T + P))
S_CMP = (slice(NC + T, 2 * NC + T), slice(0, NC))
CMP_SHIFT = P // STRIDE
CMP_SEEN = (P - L_CMP) // STRIDE + 1
assert CMP_SHIFT + CMP_SEEN == NC
assert T <= WINDOW and T // L_SEL <= N_SEL

C_Q, C_KV, C_GATE = 0, AW, AW + 6 * KV
C_ZA = C_GATE + NGATE
C_U, C_V, C_ZB = C_ZA + AW, C_ZA + AW + BW, C_ZA + AW + 2 * BW
C_MA = C_ZA + AW + 3 * BW
IN_WIDTH = C_MA + 2 * D

NB = 512
KG = 2
GE = KG * NB
RING = 4
AHEAD = 3
SL = KD // KG
YSL = AW // P // KG
LANE = 32
GATE_KT = 8
GATE_SL = KD // GATE_KT

H_CMP, H_KV, H_Q, H_U, H_V, H_ZB, H_ZA, H_M, H_Y, H_W = 0, 2, 6, 10, 14, 18, 22, 26, 42, 58
G_GATE = SL * H_U
WARM = 22
MIX_SLOT = 4


def granule_of(half):
    if half <= H_Q + 3:
        return SL * half
    if half <= H_Y:
        return SL * half + GATE_SL
    if half <= H_W:
        return granule_of(H_Y) + YSL * (half - H_Y)
    return granule_of(H_W) + SL * (half - H_W)


G_END = granule_of(H_W) + SL * (D // NB)


def buckets():
    n = np.arange(T, dtype=np.int32)
    exact = BUCKETS // 2
    nf = np.maximum(n, 1).astype(np.float32)
    large = exact + (np.log(nf / np.float32(exact)) / np.float32(np.log(MAX_DIST / exact))
                     * np.float32(BUCKETS - exact)).astype(np.int32)
    return np.where(n < exact, n, np.minimum(large, BUCKETS - 1))


def selectors():
    b = buckets()
    falling = np.zeros((BUCKETS + 1, 2 * T), np.float32)
    rising = np.zeros((BUCKETS + 1, 2 * T), np.float32)
    for i in range(2 * T):
        dist = T - 1 - i
        falling[b[dist] if dist >= 0 else BUCKETS, i] = 1.0
        dist = i - T
        rising[b[dist] if dist >= 0 else BUCKETS, i] = 1.0
    return np.concatenate([falling, rising], axis=1)


def wait(eng, sem, value):
    if isinstance(value, int) and value <= 0:
        return
    eng.wait_ge(sem, value)


def layer_kernel(nc, x_nat, x_t, rel_bias, pre_norm_t, w_in, pe_t, w1_k, w2_k, w1_v, w2_v, w_out_a,
                 sgu_norm, sgu_w_t, sgu_b_t, w_out_b, w_out, post_norm, select, any_valid, out):
    m_dram = nc.dram_tensor("merge_gates", (2 * D // NB, P, NT, NB), F32, kind="Internal").ap()
    fall_dram = nc.dram_tensor("bias_falling", (HEADS, 2 * T), F32, kind="Internal")
    bias_dram = nc.dram_tensor("bias_tiles", (HEADS, P, T), F32, kind="Internal").ap()

    with ExitStack() as ctx:
        def sb(name, shape, dt=F32, stack=ctx):
            return stack.enter_context(nc.sbuf_tensor(name, shape, dt))

        def sem(name):
            return ctx.enter_context(nc.semaphore(name))

        raw = sb("raw", [P, RING, GE])
        w_hi = sb("w_hi", [P, RING, GE], F32R)
        w_lo = sb("w_lo", [P, RING, GE], F32R)
        a_hi = sb("a_hi", [P, KD, T], F32R)
        a_lo = sb("a_lo", [P, KD, T], F32R)
        ident = sb("ident", [P, P])
        cmp_bias = sb("cmp_bias", [P, NT, NC, HEADS])
        vc = sb("vc", [LANE + NC, KV])
        gates = sb("gates", [P, NT, NGATE])
        valid = sb("valid", [P, 1])
        eps = sb("eps", [P, 1])
        sgu_bias = sb("sgu_bias", [P, BG])
        x_ss = sb("x_ss", [P, NT, 4])
        v_ss = sb("v_ss", [P, NT, 4])
        y_ss = sb("y_ss", [P, NT, D // NB])
        mean = sb("mean", [P, NT])
        root = sb("root", [P, NT])
        rstd = sb("rstd", [P, NT])
        v_rstd = sb("v_rstd", [P, NT])
        y_rstd = sb("y_rstd", [P, NT])
        neg_max = sb("neg_max", [P, NT])
        sums = sb("sums", [P, 3, NT])
        recip = sb("recip", [P, NT])
        coef = sb("coef", [P, NT])

        first = ExitStack()
        ztmp = sb("ztmp", [P, NT, NB], stack=first)
        bias = sb("bias", [P, 2, T], stack=first)
        scores = sb("scores", [P, 3 * P], stack=first)
        probs_t = sb("probs_t", [P, 3 * P], stack=first)
        q_now = sb("q_now", [P, T], stack=first)
        v_b = sb("v_b", [P, NT, BW], stack=first)
        k_t = sb("k_t", [P, 2, GROUPS, NC + T], stack=first)
        v_n = sb("v_n", [P, 2, NT, KV], stack=first)
        cmp_t = sb("cmp_t", [P, 2, GROUPS, T], stack=first)
        stage = sb("stage", [P, 2, NT, NB], stack=first)
        u_b = sb("u_b", [P, NT, BW], stack=first)
        q_o = sb("q_o", [P, HEADS, T], stack=first)
        first.close()
        xt_raw = [(u_b if s < 8 else q_o)[:].rearrange("p a b -> p (a b)")[:, (s % 8) * KG * T:(s % 8 + 1) * KG * T]
                  for s in range(SL)]
        g_pre = q_now[:, 0:KD]
        x_sq = [v_b[:, j // 2, (j % 2) * 1024:(j % 2 + 1) * 1024] for j in range(4)]
        w1 = [t[:].rearrange("p a b -> p (a b)").rearrange("p (l e) -> p l e", l=L_CMP) for t in (u_b, q_o)]
        late = [v_b[:, i, 0:GROUPS * T] for i in range(2)]
        gates_t = probs_t[0:2 * NGATE, 0:T]
        w2 = [v_b[:, i, GROUPS * T:GROUPS * T + P] for i in range(2)]
        pe = [v_b[:, i, GROUPS * T + P:GROUPS * T + P + L_CMP] for i in range(2)]
        hid = [v_b[:, i, GROUPS * T + 256:GROUPS * T + 256 + GROUPS * NC] for i in range(2)]
        sgu_wt = cmp_t[:].rearrange("p a g t -> p (a g t)").rearrange("p (g t) -> p g t", g=BG)
        sgu_g = stage[:].rearrange("p a b c -> p (a b c)")[:, 0:BW]
        pick = k_t[:].rearrange("p a g t -> p (a g t)")[0:BUCKETS + 1, 0:4 * T]
        rel = k_t[:].rearrange("p a g t -> p (a g t)")[0:BUCKETS + 1, 4 * T:4 * T + HEADS]
        falling = v_n[:].rearrange("p a b c -> p (a b c)")[0:HEADS, 0:2 * T]

        second = ExitStack()
        m_out = sb("m_out", [P, 2, NT, NB], stack=second)
        sb("pad2", [P, 512], stack=second)
        b_hi = sb("b_hi", [P, AW // P, T], F32R, stack=second)
        b_lo = sb("b_lo", [P, AW // P, T], F32R, stack=second)
        o_hi = sb("o_hi", [P, AW // P, T], F32R, stack=second)
        o_lo = sb("o_lo", [P, AW // P, T], F32R, stack=second)
        m_in = sb("m_in", [P, 2, NT, NB], stack=second)
        second.close()
        merged, part_a = m_out[:, 0], m_out[:, 1]

        third = ExitStack()
        junk = sb("junk", [P, NT, NB], stack=third)
        sb("pad3", [P, 2560 - NT * NB], stack=third)
        y = sb("y", [P, NT, D], stack=third)
        x_res = sb("x_res", [P, NT, D], stack=third)
        g_post = sb("g_post", [P, D], stack=third)
        third.close()

        acc = ctx.enter_context(nc.psum_tensor("acc", [P, 2, NT, 512], F32))
        ps_s = ctx.enter_context(nc.psum_tensor("ps_s", [P, 512], F32))
        ps_t = ctx.enter_context(nc.psum_tensor("ps_t", [P, 512], F32))
        ps_o = ctx.enter_context(nc.psum_tensor("ps_o", [P, 512], F32))
        ps_x = ctx.enter_context(nc.psum_tensor("ps_x", [P, 512], F32))

        raw_landed = [sem(f"raw_landed{s}") for s in range(RING)]
        hi_ready, lo_ready = sem("hi_ready"), sem("lo_ready")
        first_landed, first_hi, first_lo = sem("first_landed"), sem("first_hi"), sem("first_lo")
        granule_used = sem("granule_used")
        evac_act = sem("evac_act")
        xt_landed = [sem(f"xt_landed{s}") for s in range(SL)]
        g_landed, ident_made, eps_made = sem("g_landed"), sem("ident_made"), sem("eps_made")
        h_hi, h_lo = sem("h_hi"), sem("h_lo")
        xn_landed = [sem(f"xn_landed{s}") for s in range(4)]
        x_squared, x_mean, x_root, x_rstd = sem("x_squared"), sem("x_mean"), sem("x_root"), sem("x_rstd")
        pick_landed, rel_masked = sem("pick_landed"), sem("rel_masked")
        fall_done, fall_copied, fall_stored, bias_stored = (sem("fall_done"), sem("fall_copied"),
                                                            sem("fall_stored"), sem("bias_stored"))
        cmpb_done, cmpb_copied = sem("cmpb_done"), sem("cmpb_copied")
        turned, turned_copied = sem("turned"), sem("turned_copied")
        cmpw_landed = [sem("cmpw_landed_k"), sem("cmpw_landed_v")]
        pe_added, hid_done, hid_act, cmp_done, cmp_copied = (sem("pe_added"), sem("hid_done"), sem("hid_act"),
                                                            sem("cmp_done"), sem("cmp_copied"))
        gates_t_copied, gate_turned = sem("gates_t_copied"), sem("gate_turned")
        gate_act, gate_valid = sem("gate_act"), sem("gate_valid")
        small_landed = sem("small_landed")
        bias_landed = [sem("bias_landed0"), sem("bias_landed1")]
        q_ready, scores_done, biased, maxed, probs_ready = (sem("q_ready"), sem("scores_done"), sem("biased"),
                                                            sem("maxed"), sem("probs_ready"))
        probs_turned, probs_copied, pv_done, coef_steps, o_added = (sem("probs_turned"), sem("probs_copied"),
                                                                    sem("pv_done"), sem("coef_steps"), sem("o_added"))
        sguw_landed, sguw_masked, sgug_landed = sem("sguw_landed"), sem("sguw_masked"), sem("sgug_landed")
        v_squared, v_scaled = sem("v_squared"), sem("v_scaled")
        v_mean, v_root, v_rs, v_normed = sem("v_mean"), sem("v_root"), sem("v_rs"), sem("v_normed")
        mixed, gated = sem("mixed"), sem("gated")
        z_used = sem("z_used")
        o_turned, o_hi_done, o_lo_done = sem("o_turned"), sem("o_hi_done"), sem("o_lo_done")
        m_act, m_stored = sem("m_act"), [sem("m_stored0"), sem("m_stored1")]
        m_loaded = [sem("m_loaded_a"), sem("m_loaded_b")]
        merge_steps = sem("merge_steps")
        m_turned, m_hi_done, m_lo_done = sem("m_turned"), sem("m_hi_done"), sem("m_lo_done")
        y_squared, y_weighted = sem("y_squared"), sem("y_weighted")
        last_tile, last_weighted = sem("last_tile"), sem("last_weighted")
        res_landed, gpost_landed = sem("res_landed"), sem("gpost_landed")
        y_mean, y_root, y_rs, out_ready, out_stored = (sem("y_mean"), sem("y_root"), sem("y_rs"), sem("out_ready"),
                                                       sem("out_stored"))

        def gate_parts(slot):
            return w_hi[:, slot, 0:GATE_KT * 2 * NGATE].rearrange("p (k b n) -> p k b n", k=GATE_KT, b=2)

        def gate_raw(slot):
            return raw[:, slot, 0:GATE_KT * NGATE].rearrange("p (k n) -> p k n", k=GATE_KT)

        def is_gate(g):
            return isinstance(g, int) and G_GATE <= g < G_GATE + GATE_SL

        pieces = [(j, c, n) for j in range(NT)
                  for c, n in ((0, 512), (512, 1024), (1536, 1024), (2560, 1024), (3584, 512))]
        assert sum(n for _, _, n in pieces) == NT * D

        block = ctx.enter_context(nc.Block())

        @block.sync
        def _(sp):
            def load(g, slot, w, row, col, kt=KG, width=NB):
                pitch = w.shape[1]
                offset = col + row * pitch
                if not isinstance(offset, int):
                    offset = sp.snap(offset)
                wait(sp, lo_ready, g - RING + 1)
                src = bass.AP(w.tensor, offset, [[pitch, P], [P * pitch, kt], [1, width]])
                sp.dma_start(raw[:, slot, 0:kt * width].rearrange("p (a n) -> p a n", a=kt), src
                             ).then_inc(raw_landed[slot], 16)

            def half(g, w, col, n=SL):
                for s in range(n):
                    load(g + s, s % RING, w, s * KG * P, col)

            sp.dma_start(g_pre, pre_norm_t).then_inc(g_landed, 16)
            for s in range(SL):
                sp.dma_start(xt_raw[s].rearrange("p (a t) -> p a t", a=KG),
                             x_t[s * KG * P:(s + 1) * KG * P, :].rearrange("(a p) t -> p a t", p=P)
                             ).then_inc(xt_landed[s], 16)
                if s == 0:
                    for k, sem_ in enumerate((first_landed, raw_landed[0])):
                        sp.dma_start(raw[:, 0, k * NB:(k + 1) * NB], w_in[k * P:(k + 1) * P, C_KV:C_KV + NB]
                                     ).then_inc(sem_, 16)
                else:
                    load(s, s % RING, w_in, s * KG * P, C_KV)
            half(SL, w_in, C_KV + KV)
            with sp.Fori(0, 2) as i:
                for par in range(2):
                    half(granule_of(H_KV + par) + 2 * SL * i, w_in, (C_KV + 2 * KV + par * KV) + 2 * KV * i)
            with sp.Fori(0, 2) as i:
                for par in range(2):
                    half(granule_of(H_Q + par) + 2 * SL * i, w_in, (C_Q + par * NB) + 2 * NB * i)
            for s in range(GATE_SL):
                load(G_GATE + s, s % RING, w_in, s * GATE_KT * P, C_GATE, GATE_KT, NGATE)
            for h0, col in ((H_U, C_U), (H_V, C_V), (H_ZB, C_ZB), (H_ZA, C_ZA)):
                with sp.Fori(0, 2) as i:
                    for par in range(2):
                        half(granule_of(h0 + par) + 2 * SL * i, w_in, (col + par * NB) + 2 * NB * i)
            with sp.Fori(0, D // NB) as i:
                for par in range(2):
                    half(granule_of(H_M + par) + 2 * SL * i, w_in, (C_MA + par * NB) + 2 * NB * i)
            with sp.Fori(0, D // NB) as i:
                for par, w in enumerate((w_out_a, w_out_b)):
                    half(granule_of(H_Y + par) + 2 * YSL * i, w, i * NB, YSL)
            with sp.Fori(0, D // NB // 2) as i:
                for par in range(2):
                    half(granule_of(H_W + par) + 2 * SL * i, w_out, par * NB + 2 * NB * i)
            out_t = out[0].rearrange("(a p) n -> p a n", p=P)
            for k, (j, c, n) in enumerate(pieces):
                sp.wait_ge(out_ready, k + 1)
                sp.dma_start(out_t[:, j, c:c + n], y[:, j, c:c + n]).then_inc(out_stored, 16)
            sp.wait_ge(out_stored, 16 * len(pieces))

        @block.gpsimd
        def _(pool):
            pool.memset(ident[:], 0.0).then_inc(ident_made, 1)
            pool.wait_ge(ident_made, 1)
            pool.affine_select(out=ident[:], in_=ident[:], compare_op=ALU.not_equal, fill=1.0, base=0,
                               pattern=[[-1, P]], channel_multiplier=1).then_inc(ident_made, 1)
            pool.dma_start(pick, select).then_inc(pick_landed, 16)
            pool.dma_start(rel[0:BUCKETS, :], rel_bias).then_inc(pick_landed, 16)
            pool.wait_ge(h_lo, 8)
            for k in range(8):
                j, c = k % 2, k // 2
                if k >= 4:
                    pool.wait_ge(x_squared, k - 3)
                pool.dma_start(x_sq[k % 4], x_nat[j * P:(j + 1) * P, c * 1024:(c + 1) * 1024]
                               ).then_inc(xn_landed[k % 4], 16)
            pool.dma_start(valid[:], any_valid).then_inc(small_landed, 16)
            pool.dma_start(sgu_bias[:], sgu_b_t).then_inc(small_landed, 16)
            pool.wait_ge(fall_copied, 1)
            pool.dma_start(fall_dram.ap(), falling).then_inc(fall_stored, 16)
            pool.wait_ge(fall_stored, 16)
            pool.dma_start(bias_dram, bass.AP(fall_dram, P - 1, [[2 * T, HEADS], [-1, P], [1, T]])
                           ).then_inc(bias_stored, 16)
            pool.wait_ge(h_lo, KD)
            for i, (w1_d, w2_d) in enumerate(((w1_k, w2_k), (w1_v, w2_v))):
                for c in range(4):
                    pool.wait_ge(granule_used, SL + 8 * i + 2 * c)
                    pool.dma_start(w1[i][:, 8 * c:8 * c + 8, :],
                                   w1_d[8 * c * DH:8 * (c + 1) * DH, :].rearrange("(l d) e -> d l e", d=DH)
                                   ).then_inc(cmpw_landed[i], 16)
                pool.wait_ge(x_squared, 8)
                pool.dma_start(w2[i], w2_d).then_inc(cmpw_landed[i], 16)
                pool.dma_start(pe[i], pe_t[i]).then_inc(cmpw_landed[i], 16)
            pool.wait_ge(hid_done, 2)
            pool.dma_start(sgu_wt, sgu_w_t).then_inc(sguw_landed, 16)
            pool.wait_ge(bias_stored, 16)
            for h in range(2):
                pool.dma_start(bias[:, h, :], bias_dram[h]).then_inc(bias_landed[h], 16)
            pool.wait_ge(sguw_landed, 16)
            pool.affine_select(out=sgu_wt, in_=sgu_wt, compare_op=ALU.is_ge, fill=0.0, base=0,
                               pattern=[[0, BG], [1, P]], channel_multiplier=-1).then_inc(sguw_masked, 1)
            pool.wait_ge(turned_copied, 10)
            pool.tensor_copy(q_now[:], q_o[:, 0, :]).then_inc(q_ready, 1)
            pool.wait_ge(turned, 8)
            pool.dma_start(sgu_g, sgu_norm.partition_broadcast(P)).then_inc(sgug_landed, 16)
            pool.wait_ge(sgug_landed, 16)
            pool.wait_ge(turned_copied, 16)

            def head_half(sec, par, i):
                h = (4 * sec + par) + 2 * i
                half = (H_U + 4 * sec + par) + 2 * i
                cols = ds(par * NB + 2 * NB * i, NB)
                pool.wait_ge(biased, 6 * h + 6)
                if sec < 3 or i == 0:
                    pool.dma_start(bias[:, par, :], bias_dram[ds(h + 2, 1)].rearrange("a p t -> p (a t)")
                                   ).then_inc(bias_landed[par], 16)
                if sec < 3 or i == 0 or par == 0:
                    pool.tensor_copy(q_now[:], q_o[:, ds(h + 1, 1), :].rearrange("p a t -> p (a t)")
                                     ).then_inc(q_ready, 1)
                if sec == 1:
                    pool.wait_ge(v_squared, (2 * par + 2) + 4 * i)
                    for j in range(NT):
                        pool.tensor_tensor(v_b[:, j, cols], v_b[:, j, cols], sgu_g[:, cols], ALU.mult
                                           ).then_inc(v_scaled, 1)
                if sec == 2:
                    pool.wait_ge(evac_act, half + 1)
                    pool.wait_ge(mixed, 2 * BG)
                    for j in range(NT):
                        pool.tensor_tensor(u_b[:, j, cols], u_b[:, j, cols], ztmp[:, j, :], ALU.mult
                                           ).then_inc(z_used, 1)
                if sec == 3:
                    pool.wait_ge(evac_act, half + 1)
                    pool.wait_ge(o_added, 24 * (par + 1) + 48 * i)
                    for j in range(NT):
                        o4 = q_o[:, ds(4 * par + 8 * i, 4), j * DH:(j + 1) * DH]
                        pool.tensor_tensor(o4, o4, ztmp[:, j, :].rearrange("p (h d) -> p h d", h=4), ALU.mult
                                           ).then_inc(z_used, 1)

            for sec in range(3):
                with pool.Fori(0, 2) as i:
                    for par in range(2):
                        head_half(sec, par, i)
            for i in range(2):
                for par in range(2):
                    head_half(3, par, i)
            with pool.Fori(0, D // NB) as i:
                for par in range(2):
                    pool.wait_ge(m_act, (2 * par + 2) + 4 * i)
                    pool.dma_start(m_dram[ds(par + 2 * i, 1)].rearrange("c p a n -> p (c a) n"), m_out[:, par]
                                   ).then_inc(m_stored[par], 16)
            for par in range(2):
                pool.wait_ge(m_stored[par], 16 * (D // NB))

            def load_gates(c, k):
                pool.dma_start(m_in[:, k], m_dram[ds(k * (D // NB) + c, 1)].rearrange("c p a n -> p (c a) n")
                               ).then_inc(m_loaded[k], 16)

            pool.wait_ge(o_lo_done, 2 * AW // P)
            for k in range(2):
                load_gates(0, k)
            with pool.Fori(0, D // NB - 1) as c:
                pool.wait_ge(merge_steps, 5 * c + 2)
                load_gates(c + 1, 0)
                pool.wait_ge(merge_steps, 5 * c + 4)
                load_gates(c + 1, 1)
            pool.wait_ge(granule_used, granule_of(H_W))
            pool.wait_ge(merge_steps, 5 * (D // NB))
            def load_residual(cols):
                pool.dma_start(g_post[:, cols], post_norm[cols].partition_broadcast(P)).then_inc(gpost_landed, 16)
                pool.dma_start(x_res[:, :, cols], x_nat[:, cols].rearrange("(a p) n -> p a n", p=P)
                               ).then_inc(res_landed, 16)

            with pool.Fori(0, D // NB - 1) as c:
                cols = ds(c * NB, NB)
                load_residual(cols)
                pool.wait_ge(gpost_landed, 16 * c + 16)
                pool.wait_ge(y_squared, 2 * c + 2)
                for j in range(NT):
                    pool.tensor_tensor(y[:, j, cols], y[:, j, cols], g_post[:, cols],
                                       ALU.mult).then_inc(y_weighted, 1)
            load_residual(slice(D - NB, D))

        @block.scalar
        def _(act):
            def split(g, slot):
                act.wait_ge(raw_landed[slot], 16 + 4 * (g - slot))
                wait(act, granule_used, g - RING + 1)
                if is_gate(g):
                    act.activation(gate_parts(slot)[:, :, 0, :], gate_raw(slot), ACT.Copy).then_inc(hi_ready, 1)
                    return
                act.activation(w_hi[:, slot, :], raw[:, slot, :], ACT.Copy).then_inc(hi_ready, 1)

            def split_h(s):
                act.wait_ge(xt_landed[s], 16)
                for a in range(KG):
                    kt = KG * s + a
                    act.activation(a_hi[:, kt, :], xt_raw[s][:, a * T:(a + 1) * T], ACT.Copy,
                                   scale=g_pre[:, kt:kt + 1]).then_inc(h_hi, 1)

            def half_end(g_end):
                act.wait_ge(granule_used, g_end)

            def to_sbuf(dest, pair, func=ACT.Copy, sem_=None, scale=None):
                for j in range(NT):
                    ins = act.activation(dest(j), acc[:, pair, j, :], func, scale=rstd[:, j:j + 1])
                    if j == NT - 1:
                        ins.then_inc(evac_act, 1)
                    elif sem_ is not None:
                        ins.then_inc(sem_, 1)
                return ins

            def attend(k, h, par):
                for b, slot in enumerate((2, 6, 10)):
                    n = 3 * h + b
                    if k == slot:
                        act.wait_ge(maxed, 2 * n + 2)
                        parts = ((1, scores[:, 0:T]), (0, scores[:, T:T + P])) if b < 2 else \
                            tuple((j, scores[:, LANE * j:LANE * j + NC]) for j in range(NT))
                        for j, part in parts:
                            act.activation(part, part, ACT.Exp, bias=neg_max[:, j:j + 1],
                                           accum_out=sums[:, b, j:j + 1]).then_inc(probs_ready, 1)
                    if k == slot + 2:
                        act.wait_ge(probs_turned, n + 1)
                        rows, width = (P, 3 * P) if b < 2 else (LANE + NC, P)
                        act.activation(probs_t[0:rows, 0:width], ps_t[0:rows, 0:width], ACT.Copy
                                       ).then_inc(probs_copied, 1)

            act.wait_ge(eps_made, 1)
            act.activation(root[:, 0:1], eps[:], ACT.Copy)
            act.wait_ge(g_landed, 16)
            split_h(0)
            act.wait_ge(first_landed, 16)
            act.activation(w_hi[:, 0, 0:NB], raw[:, 0, 0:NB], ACT.Copy).then_inc(first_hi, 1)
            act.wait_ge(raw_landed[0], 16)
            act.activation(w_hi[:, 0, NB:GE], raw[:, 0, NB:GE], ACT.Copy).then_inc(hi_ready, 1)
            for s in range(1, AHEAD):
                split_h(s)
                split(s, s)
            for par in range(2):
                for k in range(SL):
                    if par == 0 and k + AHEAD < SL:
                        split_h(k + AHEAD)
                    split(SL * par + k + AHEAD, (k + AHEAD) % RING)
                if par == 0:
                    act.wait_ge(x_mean, 1)
                    act.wait_ge(eps_made, 1)
                    act.activation(root[:], mean[:], ACT.Sqrt, bias=eps[:, 0:1], scale=1.0 / D).then_inc(x_root, 1)
                    act.wait_ge(x_rstd, 1)
                half_end(SL * (par + 1))
                to_sbuf(lambda j: stage[:, par, j, :], par)
            act.wait_ge(fall_stored, 16)
            with act.Fori(0, 2) as i:
                for par in range(2):
                    g0 = granule_of(H_KV + par) + 2 * SL * i
                    for k in range(SL):
                        split(g0 + k + AHEAD, (k + AHEAD) % RING)
                    half_end(g0 + SL)
                    if par == 0:
                        act.wait_ge(turned, 2 + i)
                        to_sbuf(lambda j: stage[:, 0, j, :], 0)
                    else:
                        to_sbuf(lambda j: v_n[:, ds(i, 1), j, :].rearrange("p a n -> p (a n)"), 1)
            for kv in range(2):
                act.wait_ge(hid_done, kv + 1)
                act.activation(hid[kv], (ps_x if kv == 0 else ps_s)[:, 0:GROUPS * NC], ACT.Silu).then_inc(hid_act, 1)
            for i in range(2):
                for par in range(2):
                    g0 = granule_of(H_Q + par) + 2 * SL * i
                    for k in range(SL):
                        split(g0 + k + AHEAD, (k + AHEAD) % RING)
                    half_end(g0 + SL)
                    act.wait_ge(turned, (4 + par) + i)
                    to_sbuf(lambda j: stage[:, par, j, :], par)
            for s in range(GATE_SL):
                split(G_GATE + s + AHEAD, (s + AHEAD) % RING)
            act.wait_ge(granule_used, G_GATE + GATE_SL)
            act.activation(gates_t, ps_x[0:2 * NGATE, 0:T], ACT.Copy).then_inc(gates_t_copied, 1)
            act.wait_ge(gate_turned, 1)
            for j in range(NT):
                act.activation(gates[:, j, :], ps_x[:, T + j * NGATE:T + (j + 1) * NGATE], ACT.Sigmoid,
                               scale=rstd[:, j:j + 1]).then_inc(gate_act, 1)

            def head_half(sec, par, i, dest, func):
                g0 = granule_of(H_U + 4 * sec + par) + 2 * SL * i
                for k in range(SL):
                    split(g0 + k + AHEAD, (k + AHEAD) % RING)
                    if isinstance(g0, int) and g0 == granule_of(H_ZB) and k == 0:
                        act.wait_ge(v_mean, 1)
                        act.activation(root[:], mean[:], ACT.Sqrt, bias=eps[:, 0:1], scale=1.0 / BW
                                       ).then_inc(v_root, 1)
                    attend(k, (4 * sec + par) + 2 * i, par)
                half_end(g0 + SL)
                if sec >= 2:
                    wait(act, z_used, (8 * (sec - 2) + 2 * par) + 4 * i)
                to_sbuf(dest, par, func)

            for sec, dest in enumerate((u_b, v_b)):
                with act.Fori(0, 2) as i:
                    for par in range(2):
                        cols = ds(par * NB + 2 * NB * i, NB)
                        head_half(sec, par, i, lambda j: dest[:, j, cols], ACT.Gelu_apprx_tanh)
            for i in range(2):
                for par in range(2):
                    head_half(2, par, i, lambda j: ztmp[:, j, :], ACT.Silu)
            with act.Fori(0, 2) as i:
                for par in range(2):
                    head_half(3, par, i, lambda j: ztmp[:, j, :], ACT.Silu)

            def merge_gate_half(i, turn):
                for par in range(2):
                    g0 = granule_of(H_M + par) + 2 * SL * i
                    for k in range(SL):
                        split(g0 + k + AHEAD, (k + AHEAD) % RING)
                        if turn is not None and k > 0:
                            turn(SL * par + k - 1)
                    half_end(g0 + SL)
                    if turn is not None:
                        turn(SL * par + SL - 1)
                        act.wait_ge(z_used, 16)
                    else:
                        act.wait_ge(m_stored[par], 16 * i)
                    for j in range(NT):
                        ins = act.activation(m_out[:, par, j, :], acc[:, par, j, :], ACT.Sigmoid,
                                             scale=rstd[:, j:j + 1])
                        ins.then_inc(m_act, 1)

            def turn_hi(q):
                act.wait_ge(o_turned, q + 1)
                dest = (b_hi if q < 16 else o_hi)[:, q % 16, :]
                act.activation(dest, (ps_s if q % 2 == 0 else ps_t)[:, 0:T], ACT.Copy).then_inc(o_hi_done, 1)

            merge_gate_half(0, turn_hi)
            with act.Fori(1, D // NB) as i:
                merge_gate_half(i, None)

            def merged_hi(c, q):
                act.wait_ge(m_turned, 4 * c + q + 1)
                act.activation(a_hi[:, ds(4 * c + q, 1), :].rearrange("p a t -> p (a t)"),
                               (ps_s if q % 2 == 0 else ps_t)[:, 0:T], ACT.Copy).then_inc(m_hi_done, 1)

            def y_half(c, first_):
                g0 = granule_of(H_Y) + 2 * YSL * c
                for k in range(2 * YSL):
                    split(g0 + k + AHEAD, (k + AHEAD) % RING)
                    if not first_ and 2 <= k < 6:
                        merged_hi(c - 1, k - 2)

            y_half(0, True)
            with act.Fori(1, D // NB) as c:
                y_half(c, False)

            def w_half(c, par, last_merged=False):
                g0 = granule_of(H_W) + SL * c
                for k in range(SL):
                    split(g0 + k + AHEAD, (k + AHEAD) % RING)
                    if last_merged and 2 <= k < 6:
                        merged_hi(D // NB - 1, k - 2)
                half_end(g0 + SL)
                if last_merged:
                    act.wait_ge(merge_steps, 5 * (D // NB))
                for j in range(NT):
                    act.activation(y[:, j, ds(c * NB, NB)], acc[:, par, j, :], ACT.Copy)
                    wait(act, y_squared, 2 * c + (j - 1))
                    act.activation(junk[:, j, :], acc[:, par, j, :], ACT.Square,
                                   accum_out=y_ss[:, j, ds(c, 1)]).then_inc(y_squared, 1)

            w_half(0, 0, last_merged=True)
            w_half(1, 1)
            with act.Fori(1, D // NB // 2 - 1) as i:
                for par in range(2):
                    w_half(2 * i + par, par)
            w_half(D // NB - 2, 0)
            last = D // NB - 1
            for k in range(SL - AHEAD):
                split(granule_of(H_W) + SL * last + k + AHEAD, (k + AHEAD) % RING)
            act.activation(y_rstd[:, 0:1], eps[:], ACT.Sqrt)
            for j in range(NT):
                act.wait_ge(last_tile, j + 1)
                act.wait_ge(y_squared, 2 * last + j - 1)
                act.activation(junk[:, j, :], acc[:, 1, j, :], ACT.Square,
                               accum_out=y_ss[:, j, last:last + 1]).then_inc(y_squared, 1)
                act.wait_ge(y_mean, j + 1)
                act.activation(root[:, j:j + 1], mean[:, j:j + 1], ACT.Sqrt, bias=eps[:, 0:1], scale=1.0 / D
                               ).then_inc(y_root, 1)

        @block.vector
        def _(dve):
            def split(g, slot):
                dve.wait_ge(hi_ready, g + 1)
                if is_gate(g):
                    hi, lo = (gate_parts(slot)[:, :, b, :] for b in range(2))
                    dve.tensor_tensor(lo, gate_raw(slot), hi.bitcast(F32), ALU.subtract).then_inc(lo_ready, 1)
                    return
                dve.tensor_tensor(w_lo[:, slot, :], raw[:, slot, :], w_hi[:, slot, :].bitcast(F32), ALU.subtract
                                  ).then_inc(lo_ready, 1)

            def split_h(s):
                for a in range(KG):
                    kt = KG * s + a
                    dve.wait_ge(h_hi, kt + 1)
                    dve.scalar_tensor_tensor(out=a_lo[:, kt, :], in0=xt_raw[s][:, a * T:(a + 1) * T],
                                             scalar=g_pre[:, kt:kt + 1], in1=a_hi[:, kt, :].bitcast(F32),
                                             op0=ALU.mult, op1=ALU.subtract).then_inc(h_lo, 1)

            def square_x(k):
                dve.wait_ge(xn_landed[k % 4], 16 * (k // 4 + 1))
                dve.tensor_tensor_reduce(x_sq[k % 4], x_sq[k % 4], x_sq[k % 4], 1.0, 0.0, ALU.mult, ALU.add,
                                         x_ss[:, k % 2, k // 2:k // 2 + 1]).then_inc(x_squared, 1)

            def turned_to(dest, m):
                dve.wait_ge(turned, m + 1)
                for a, ps in enumerate((ps_t, ps_o)):
                    dve.tensor_copy(dest[:, 2 * a:2 * a + 2, :], ps[:].rearrange("p (g t) -> p g t", g=2)
                                    ).then_inc(turned_copied, 1)

            def attend(k, h, par, sec, i):
                for b, slot in enumerate((1, 5, 9)):
                    n = 3 * h + b
                    if k == slot:
                        if b == 0:
                            dve.wait_ge(bias_landed[par], (32 * sec + 16) + 16 * i)
                        dve.wait_ge(scores_done, n + 1)
                        if not (sec == 0 and par == 0 and b == 0):
                            dve.wait_ge(probs_turned, n)
                        if b < 2:
                            for dst, src, first_key in ((slice(0, T), S_LATE[b], 0), (slice(T, T + P), S_EARLY[b], P)):
                                dve.scalar_tensor_tensor(out=scores[:, dst], in0=ps_s[:, src], scalar=SCALE,
                                                         in1=bias[:, par, first_key:T], op0=ALU.mult, op1=ALU.add
                                                         ).then_inc(biased, 1)
                            dve.wait_ge(biased, 2 * n + 2)
                            dve.tensor_reduce(neg_max[:, 1:2], scores[:, 0:T], AX.X, ALU.max, negate=True
                                              ).then_inc(maxed, 1)
                            dve.tensor_reduce(neg_max[:, 0:1], scores[:, T:T + P], AX.X, ALU.max, negate=True
                                              ).then_inc(maxed, 1)
                        else:
                            for j in range(NT):
                                dve.scalar_tensor_tensor(
                                    out=scores[:, LANE * j:LANE * j + NC], in0=ps_s[:, S_CMP[j]], scalar=SCALE,
                                    in1=cmp_bias[:, j, :, ds(h, 1)].rearrange("p n a -> p (n a)"),
                                    op0=ALU.mult, op1=ALU.add).then_inc(biased, 1)
                            both = scores[:, 0:NT * LANE].rearrange("p (j n) -> p j n", j=NT)[:, :, 0:NC]
                            dve.wait_ge(biased, 2 * n + 2)
                            dve.tensor_reduce(neg_max[:], both, AX.X, ALU.max, negate=True).then_inc(maxed, 2)
                    if k == slot + 5:
                        dve.wait_ge(probs_ready, 2 * n + 2)
                        dve.reciprocal(recip[:], sums[:, b, :]).then_inc(coef_steps, 1)
                        dve.wait_ge(coef_steps, 2 * n + 1)
                        dve.tensor_tensor(coef[:], recip[:],
                                          gates[:, :, ds(3 * h + GATE[b], 1)].rearrange("p j a -> p (j a)"), ALU.mult
                                          ).then_inc(coef_steps, 1)
                        dve.wait_ge(coef_steps, 2 * n + 2)
                        dve.wait_ge(pv_done, n + 1)
                        for j in range(NT):
                            pv = (ps_t if b == 2 and j == 1 else ps_o)[:, j * DH:(j + 1) * DH]
                            o_h = q_o[:, ds(h, 1), j * DH:(j + 1) * DH].rearrange("p a d -> p (a d)")
                            if b == 0:
                                dve.tensor_scalar(o_h, pv, coef[:, j:j + 1], None, ALU.mult
                                                  ).then_inc(o_added, 1)
                            else:
                                dve.wait_ge(o_added, 2 * n)
                                dve.scalar_tensor_tensor(out=o_h, in0=pv, scalar=coef[:, j:j + 1], in1=o_h, op0=ALU.mult,
                                                         op1=ALU.add).then_inc(o_added, 1)

            def mix(m):
                dve.wait_ge(gated, m + 1)
                for q in range(4):
                    grp, j = 2 * m + q // 2, q % 2
                    cols = slice(grp * P, (grp + 1) * P)
                    dve.scalar_tensor_tensor(out=u_b[:, j, cols], in0=ps_x[:, q * P:(q + 1) * P],
                                             scalar=sgu_bias[:, grp:grp + 1], in1=u_b[:, j, cols],
                                             op0=ALU.add, op1=ALU.mult).then_inc(mixed, 1)

            dve.memset(eps[:], EPS).then_inc(eps_made, 1)
            dve.memset(rel[BUCKETS:BUCKETS + 1, :], MASKED).then_inc(rel_masked, 1)
            split_h(0)
            for cols, hi_there, lo_there in ((slice(0, NB), first_hi, first_lo), (slice(NB, GE), hi_ready, lo_ready)):
                dve.wait_ge(hi_there, 1)
                dve.tensor_tensor(w_lo[:, 0, cols], raw[:, 0, cols], w_hi[:, 0, cols].bitcast(F32), ALU.subtract
                                  ).then_inc(lo_there, 1)
            for s in range(1, AHEAD):
                split_h(s)
                split(s, s)
            for par in range(2):
                for k in range(SL):
                    if par == 0 and k + AHEAD < SL:
                        split_h(k + AHEAD)
                    split(SL * par + k + AHEAD, (k + AHEAD) % RING)
                    if par == 0 and k == 3:
                        dve.wait_ge(fall_done, 1)
                        dve.tensor_copy(falling, ps_s[0:HEADS, :]).then_inc(fall_copied, 1)
                        dve.wait_ge(cmpb_done, 1)
                        dve.tensor_copy(cmp_bias[:, 1].rearrange("p n h -> p (n h)"), ps_x[:, 0:NC * HEADS]
                                        ).then_inc(cmpb_copied, 1)
                        dve.tensor_copy(cmp_bias[:, 0, 0:CMP_SEEN].rearrange("p n h -> p (n h)"),
                                        ps_x[:, CMP_SHIFT * HEADS:NC * HEADS]).then_inc(cmpb_copied, 1)
                        dve.memset(cmp_bias[:, 0, CMP_SEEN:NC], MASKED).then_inc(cmpb_copied, 1)
                    if par == 0 and k >= 8:
                        square_x(k - 8)
                    if par == 1 and k == 6:
                        turned_to(cmp_t[:, 0], 0)
                if par == 0:
                    dve.wait_ge(x_squared, 8)
                    dve.tensor_reduce(mean[:], x_ss[:], AX.X, ALU.add).then_inc(x_mean, 1)
                    dve.wait_ge(x_root, 1)
                    dve.reciprocal(rstd[:], root[:]).then_inc(x_rstd, 1)

            def add_embedding(kv, half_):
                dve.wait_ge(turned_copied, 4)
                dve.wait_ge(cmpw_landed[kv], 96)
                kvt = cmp_t[:, kv].rearrange("p g (j r) -> p (g j) r", r=STRIDE)
                dest = late[kv].rearrange("p (j r) -> p j r", r=STRIDE) if half_ else kvt
                emb = pe[kv][:, half_ * STRIDE:(half_ + 1) * STRIDE].rearrange("p (a r) -> p a r", a=1)
                dve.tensor_tensor(dest, kvt, emb.broadcast_to([P, GROUPS * T // STRIDE, STRIDE]), ALU.add
                                  ).then_inc(pe_added, 1)

            for i in range(2):
                for par in range(2):
                    g0 = granule_of(H_KV + par) + 2 * SL * i
                    for k in range(SL):
                        split(g0 + k + AHEAD, (k + AHEAD) % RING)
                        if i == 0 and par == 0 and k == 2:
                            turned_to(cmp_t[:, 1], 1)
                        if i == 0 and par == 1 and k in (6, 8, 10, 12):
                            add_embedding((k - 6) // 4, 1 - (k - 6) // 2 % 2)
                        if par == 1 and k == 2:
                            turned_to(k_t[:, i, :, NC:NC + T], 2 + i)
            for i in range(2):
                for par in range(2):
                    g0 = granule_of(H_Q + par) + 2 * SL * i
                    for k in range(SL):
                        split(g0 + k + AHEAD, (k + AHEAD) % RING)
                        if i == 0 and par == 0 and k == 2:
                            dve.wait_ge(cmp_done, 1)
                            dve.tensor_copy(k_t[:, 1, :, 0:NC],
                                            ps_t[:, 0:GROUPS * NC].rearrange("p (g n) -> p g n", g=GROUPS)
                                            ).then_inc(cmp_copied, 1)
                        if i == 0 and par == 0 and k == 3:
                            dve.wait_ge(cmp_done, 2)
                            for j in range(NT):
                                dve.tensor_copy(vc[LANE * j:LANE * j + NC, :], ps_o[LANE * j:LANE * j + NC, :]
                                                ).then_inc(cmp_copied, 1)
                        if par == 1 and k == 2:
                            turned_to(q_o[:, 8 * i:8 * i + 4, :], 4 + 2 * i)
                        if i == 1 and par == 0 and k == 2:
                            turned_to(q_o[:, 4:8, :], 5)
            for s in range(GATE_SL):
                split(G_GATE + s + AHEAD, (s + AHEAD) % RING)
            turned_to(q_o[:, 12:16, :], 7)
            dve.wait_ge(gate_act, 2)
            dve.wait_ge(small_landed, 32)
            own = gates[:, 0, :].rearrange("p (h b) -> p h b", b=3)[:, :, 0]
            dve.tensor_scalar(own, own, valid[:, 0:1], None, ALU.mult).then_inc(gate_valid, 1)
            dve.wait_ge(gate_valid, 1)
            with dve.Fori(0, 2) as i:
                for par in range(2):
                    g0 = granule_of(H_U + par) + 2 * SL * i
                    for k in range(SL):
                        split(g0 + k + AHEAD, (k + AHEAD) % RING)
                        attend(k, par + 2 * i, par, 0, i)
            for half in range(4):
                for k in range(SL):
                    split(granule_of(H_V + half) + k + AHEAD, (k + AHEAD) % RING)
                    attend(k, 4 + half, half % 2, 1, half // 2)
                dve.wait_ge(evac_act, H_V + half + 1)
                for j in range(NT):
                    v_half = v_b[:, j, half * NB:(half + 1) * NB]
                    dve.tensor_tensor_reduce(ztmp[:, j, :], v_half, v_half, 1.0, 0.0, ALU.mult, ALU.add,
                                             v_ss[:, j, half:half + 1]).then_inc(v_squared, 1)

            def v_norm(k):
                if k == 0:
                    dve.wait_ge(v_squared, 8)
                    dve.tensor_reduce(mean[:], v_ss[:], AX.X, ALU.add).then_inc(v_mean, 1)
                if k == 1:
                    dve.wait_ge(v_root, 1)
                    dve.reciprocal(v_rstd[:], root[:]).then_inc(v_rs, 1)
                if k in (2, 3):
                    dve.wait_ge(v_rs, 1)
                    dve.wait_ge(v_scaled, 8)
                    j = k - 2
                    dve.tensor_scalar(v_b[:, j, :], v_b[:, j, :], v_rstd[:, j:j + 1], None, ALU.mult
                                      ).then_inc(v_normed, 1)

            for half in range(4):
                sec, par = 2, half % 2
                g0 = granule_of(H_ZB + half)
                for k in range(SL):
                    split(g0 + k + AHEAD, (k + AHEAD) % RING)
                    attend(k, 8 + half, par, sec, half // 2)
                    if half == 0:
                        v_norm(k)
                    if half == 0 and MIX_SLOT < k <= MIX_SLOT + BG // 2:
                        mix(k - MIX_SLOT - 1)
            with dve.Fori(0, 2) as i:
                for par in range(2):
                    g0 = granule_of(H_ZA + par) + 2 * SL * i
                    for k in range(SL):
                        split(g0 + k + AHEAD, (k + AHEAD) % RING)
                        attend(k, (12 + par) + 2 * i, par, 3, i)

            def turn_lo(q):
                dve.wait_ge(o_hi_done, q + 1)
                hi, lo = (b_hi, b_lo) if q < 16 else (o_hi, o_lo)
                dve.tensor_tensor(lo[:, q % 16, :], (ps_s if q % 2 == 0 else ps_t)[:, 0:T],
                                  hi[:, q % 16, :].bitcast(F32), ALU.subtract).then_inc(o_lo_done, 1)

            for par in range(2):
                g0 = granule_of(H_M + par)
                for k in range(SL):
                    split(g0 + k + AHEAD, (k + AHEAD) % RING)
                    if k > 0:
                        turn_lo(SL * par + k - 1)
                turn_lo(SL * par + SL - 1)
            with dve.Fori(1, D // NB) as i:
                for par in range(2):
                    g0 = granule_of(H_M + par) + 2 * SL * i
                    for k in range(SL):
                        split(g0 + k + AHEAD, (k + AHEAD) % RING)

            def merged_lo(c, q):
                dve.wait_ge(m_hi_done, 4 * c + q + 1)
                kt = ds(4 * c + q, 1)
                dve.tensor_tensor(a_lo[:, kt, :].rearrange("p a t -> p (a t)"), (ps_s if q % 2 == 0 else ps_t)[:, 0:T],
                                  a_hi[:, kt, :].rearrange("p a t -> p (a t)").bitcast(F32), ALU.subtract
                                  ).then_inc(m_lo_done, 1)

            def y_half(c, first_):
                g0 = granule_of(H_Y) + 2 * YSL * c
                for k in range(2 * YSL):
                    split(g0 + k + AHEAD, (k + AHEAD) % RING)
                    if not first_ and 2 <= k < 6:
                        merged_lo(c - 1, k - 2)
                    if k == YSL:
                        dve.wait_ge(m_loaded[0], 16 * c + 16)
                        dve.wait_ge(granule_used, g0 + YSL)
                        for j in range(NT):
                            dve.tensor_tensor(part_a[:, j, :], acc[:, 0, j, :], m_in[:, 0, j, :], ALU.mult
                                              ).then_inc(merge_steps, 1)
                dve.wait_ge(m_loaded[1], 16 * c + 16)
                dve.wait_ge(granule_used, g0 + 2 * YSL)
                if not first_:
                    dve.wait_ge(m_turned, 4 * c)
                for j in range(NT):
                    dve.tensor_tensor(merged[:, j, :], acc[:, 1, j, :], m_in[:, 1, j, :], ALU.mult
                                      ).then_inc(merge_steps, 1)
                dve.wait_ge(merge_steps, 5 * c + 4)
                dve.tensor_tensor(merged, merged, part_a, ALU.add).then_inc(merge_steps, 1)

            y_half(0, True)
            with dve.Fori(1, D // NB) as c:
                y_half(c, False)

            g0 = granule_of(H_W)
            for k in range(SL):
                split(g0 + k + AHEAD, (k + AHEAD) % RING)
                if 2 <= k < 6:
                    merged_lo(D // NB - 1, k - 2)
            with dve.Fori(1, D // NB - 1) as c:
                for k in range(SL):
                    split(g0 + SL * c + k + AHEAD, (k + AHEAD) % RING)
            last = D // NB - 1
            for k in range(SL - AHEAD):
                split(g0 + SL * last + k + AHEAD, (k + AHEAD) % RING)
            dve.wait_ge(gpost_landed, 16 * (D // NB))
            dve.wait_ge(res_landed, 16 * (D // NB))
            for j, c, n in pieces:
                if c == 0:
                    dve.wait_ge(y_squared, 2 * last + j + 1)
                    dve.tensor_reduce(mean[:, j:j + 1], y_ss[:, j, :], AX.X, ALU.add).then_inc(y_mean, 1)
                    dve.wait_ge(y_root, j + 1)
                    dve.reciprocal(y_rstd[:, j:j + 1], root[:, j:j + 1]).then_inc(y_rs, 1)
                    dve.wait_ge(y_rs, j + 1)
                dve.wait_ge(y_weighted, 2 * min((c + n) // NB, last))
                if c + n > last * NB:
                    dve.tensor_tensor(y[:, j, last * NB:], acc[:, 1, j, :], g_post[:, last * NB:], ALU.mult
                                      ).then_inc(last_weighted, 1)
                    dve.wait_ge(last_weighted, j + 1)
                dve.scalar_tensor_tensor(out=y[:, j, c:c + n], in0=y[:, j, c:c + n], scalar=y_rstd[:, j:j + 1],
                                         in1=x_res[:, j, c:c + n], op0=ALU.mult, op1=ALU.add
                                         ).then_inc(out_ready, 1)

        @block.tensor
        def _(pe_):
            def granule(g, slot, pair, s, n, hi, lo):
                pe_.wait_ge(lo_ready, g + 1)
                for a in range(KG):
                    kt = KG * s + a
                    wh, wl = (w[:, slot, a * NB:(a + 1) * NB] for w in (w_hi, w_lo))
                    for j in range(NT):
                        tok = slice(j * P, (j + 1) * P)
                        dst = acc[:, pair, j, :]
                        pe_.matmul(dst, hi[:, kt, tok], wh, start=(kt == 0), stop=False)
                        pe_.matmul(dst, hi[:, kt, tok], wl, start=False, stop=False)
                        last = pe_.matmul(dst, lo[:, kt, tok], wh, start=False, stop=(kt == KG * n - 1))
                last.then_inc(granule_used, 1)

            assert KG == 2

            def early_granule(s):
                pe_.wait_ge(h_hi, KG * (s + 1))
                for a in range(KG):
                    if s == 0:
                        pe_.wait_ge((first_hi, hi_ready)[a], 1)
                    else:
                        pe_.wait_ge(hi_ready, s + 1)
                    for j in range(NT):
                        pe_.matmul(acc[:, 0, j, :], a_hi[:, KG * s + a, j * P:(j + 1) * P],
                                   w_hi[:, s, a * NB:(a + 1) * NB], start=(s == 0 and a == 0), stop=False)
                pe_.wait_ge(h_lo, KG * (s + 1))
                for a in range(KG):
                    if s == 0:
                        pe_.wait_ge((first_lo, lo_ready)[a], 1)
                    else:
                        pe_.wait_ge(lo_ready, s + 1)
                    wh, wl = (w[:, s, a * NB:(a + 1) * NB] for w in (w_hi, w_lo))
                    kt = KG * s + a
                    for j in range(NT):
                        tok = slice(j * P, (j + 1) * P)
                        pe_.matmul(acc[:, 0, j, :], a_hi[:, kt, tok], wl, start=False, stop=False)
                        last = pe_.matmul(acc[:, 0, j, :], a_lo[:, kt, tok], wh, start=False, stop=False)
                last.then_inc(granule_used, 1)

            def last_granules():
                for j in range(NT):
                    for s in range(SL - RING, SL):
                        if j == 0:
                            pe_.wait_ge(lo_ready, G_END - SL + s + 1)
                        for a in range(KG):
                            kt = KG * s + a
                            wh, wl = (w[:, s % RING, a * NB:(a + 1) * NB] for w in (w_hi, w_lo))
                            tok = slice(j * P, (j + 1) * P)
                            pe_.matmul(acc[:, 1, j, :], a_hi[:, kt, tok], wh, start=False, stop=False)
                            pe_.matmul(acc[:, 1, j, :], a_hi[:, kt, tok], wl, start=False, stop=False)
                            last = pe_.matmul(acc[:, 1, j, :], a_lo[:, kt, tok], wh, start=False,
                                              stop=(kt == KD - 1))
                    last.then_inc(last_tile, 1)

            def transposes(par):
                for grp in range(GROUPS):
                    for j in range(NT):
                        ps = (ps_t, ps_o)[grp // 2]
                        col = (grp % 2) * T + j * P
                        last = pe_.transpose(ps[:, col:col + P], stage[:, par, j, grp * P:(grp + 1) * P], ident[:])
                last.then_inc(turned, 1)

            def attend(k, h, sec, par):
                for b, slot in enumerate((0, 4, 8)):
                    n = 3 * h + b
                    first_ = sec == 0 and par == 0 and b == 0
                    if k == slot and b < 2:
                        if b == 0:
                            pe_.wait_ge(q_ready, h + 1)
                        if not first_:
                            pe_.wait_ge(biased, 2 * n)
                        if b == 0:
                            pe_.matmul(ps_s[:, S_LATE[0]], q_now[:, P:T], k_t[:, 0, sec, NC:], start=True, stop=True)
                            pe_.matmul(ps_s[:, S_EARLY[0]], q_now[:, 0:P], k_t[:, 0, sec, NC:NC + P],
                                       start=True, stop=True).then_inc(scores_done, 1)
                        else:
                            pe_.matmul(ps_s[:, 0:NC + T], q_now[:, P:T], k_t[:, 1, sec, :], start=True, stop=True)
                            pe_.matmul(ps_s[:, NC + T:2 * NC + T + P], q_now[:, 0:P], k_t[:, 1, sec, 0:NC + P],
                                       start=True, stop=True).then_inc(scores_done, 2)
                    if k == slot + 3:
                        pe_.wait_ge(probs_ready, 2 * n + 2)
                        if first_:
                            pe_.wait_ge(turned_copied, 16)
                        else:
                            pe_.wait_ge(probs_copied, n)
                        if b < 2:
                            for c in range(3):
                                last = pe_.transpose(ps_t[:, c * P:(c + 1) * P], scores[:, c * P:(c + 1) * P],
                                                     ident[:])
                        else:
                            last = pe_.transpose(ps_t[:, 0:P], scores[:, 0:P], ident[:])
                        last.then_inc(probs_turned, 1)
                    if k == slot + 5:
                        pe_.wait_ge(probs_copied, n + 1)
                        if not first_:
                            pe_.wait_ge(o_added, 2 * n)
                        if b < 2:
                            v = v_n[:, b, :, sec * DH:(sec + 1) * DH]
                            pe_.matmul(ps_o[:, 0:DH], probs_t[:, T:T + P], v[:, 0, :], start=True, stop=True)
                            pe_.matmul(ps_o[:, DH:2 * DH], probs_t[:, 0:P], v[:, 0, :], start=True, stop=False)
                            last = pe_.matmul(ps_o[:, DH:2 * DH], probs_t[:, P:T], v[:, 1, :], start=False,
                                              stop=True)
                        else:
                            for j in range(NT):
                                rows = slice(LANE * j, LANE * j + NC)
                                last = pe_.matmul((ps_o, ps_t)[j][:, j * DH:(j + 1) * DH], probs_t[rows, 0:P],
                                                  vc[rows, sec * DH:(sec + 1) * DH], start=True, stop=True)
                        last.then_inc(pv_done, 1)
                if k == SL - 1:
                    pe_.wait_ge(o_added, 6 * h + 6)

            pe_.wait_ge(ident_made, 2)
            for _warm in range(WARM):
                pe_.transpose(ps_t[:, 0:P], ident[:], ident[:])
            for par in range(2):
                for s in range(SL):
                    if par == 0 and s < AHEAD:
                        early_granule(s)
                    else:
                        if par == 0:
                            pe_.wait_ge(h_lo, KG * (s + 1))
                        granule(SL * par + s, s % RING, par, s, SL, a_hi, a_lo)
                    if par == 0 and s == 1:
                        pe_.wait_ge(rel_masked, 1)
                        pe_.wait_ge(pick_landed, 32)
                        pe_.matmul(ps_s[0:HEADS, :], rel, pick[:, 0:2 * T], start=True, stop=True
                                   ).then_inc(fall_done, 1)
                        for n in range(NC):
                            off = 2 * T + T + P - STRIDE * n - (L_CMP - 1)
                            last = pe_.matmul(ps_x[:, n * HEADS:(n + 1) * HEADS], pick[:, off:off + P], rel,
                                              start=True, stop=True)
                        last.then_inc(cmpb_done, 1)
                    if par == 1 and s == 5:
                        pe_.wait_ge(evac_act, 1)
                        transposes(0)
            for i in range(2):
                for par in range(2):
                    pe_.wait_ge(evac_act, (H_KV + par - 1) + 2 * i)
                    for s in range(SL):
                        granule((granule_of(H_KV + par) + s) + 2 * SL * i, s % RING, par, s, SL, a_hi, a_lo)
                        if i == 0 and par == 0 and s == 1:
                            pe_.wait_ge(evac_act, 2)
                            pe_.wait_ge(turned_copied, 2)
                            transposes(1)
                        if par == 1 and s == 1:
                            pe_.wait_ge(evac_act, (H_KV + 1) + 2 * i)
                            pe_.wait_ge(turned_copied, 4 + 2 * i)
                            transposes(0)
            for kv, ps in enumerate((ps_x, ps_s)):
                pe_.wait_ge(cmpw_landed[kv], 96)
                pe_.wait_ge(pe_added, 2 * kv + 2)
                pe_.wait_ge(*((cmpb_copied, 2), (fall_copied, 1))[kv])
                for l in range(L_CMP):
                    src = cmp_t[:, kv].rearrange("p g t -> p (g t)") if l < STRIDE else late[kv]
                    src = src.rearrange("p (g j r) -> p g j r", g=GROUPS, r=STRIDE)
                    j0 = l // STRIDE
                    last = pe_.matmul(ps[:, 0:GROUPS * NC], w1[kv][:, l, :], src[:, :, j0:j0 + NC, l % STRIDE],
                                      start=(l == 0), stop=(l == L_CMP - 1))
                last.then_inc(hid_done, 1)

            def compress_k():
                pe_.wait_ge(turned_copied, 8)
                pe_.wait_ge(hid_act, 1)
                pe_.matmul(ps_t[:, 0:GROUPS * NC], w2[0], hid[0], start=True, stop=True).then_inc(cmp_done, 1)

            def compress_v():
                pe_.wait_ge(hid_act, 2)
                for j in range(NT):
                    for grp in range(GROUPS):
                        last = pe_.matmul(ps_o[LANE * j:LANE * j + NC, grp * DH:(grp + 1) * DH],
                                          hid[1][:, grp * NC:(grp + 1) * NC], w2[1], start=True, stop=True)
                last.then_inc(cmp_done, 1)

            for i in range(2):
                for par in range(2):
                    pe_.wait_ge(evac_act, (H_Q + par - 1) + 2 * i)
                    for s in range(SL):
                        granule((granule_of(H_Q + par) + s) + 2 * SL * i, s % RING, par, s, SL, a_hi, a_lo)
                        if i == 0 and par == 0 and s == 1:
                            compress_k()
                        if i == 0 and par == 0 and s == 2:
                            compress_v()
                        if i == 1 and par == 0 and s == 1:
                            pe_.wait_ge(evac_act, H_Q + 2)
                            pe_.wait_ge(turned_copied, 10)
                            transposes(1)
                        if par == 1 and s == 1:
                            pe_.wait_ge(evac_act, (H_Q + 1) + 2 * i)
                            if i == 0:
                                pe_.wait_ge(cmp_copied, 3)
                            else:
                                pe_.wait_ge(turned_copied, 12)
                            transposes(0)
            pe_.wait_ge(hid_act, 1)
            for s in range(GATE_SL):
                pe_.wait_ge(lo_ready, G_GATE + s + 1)
                for a in range(GATE_KT):
                    kt = GATE_KT * s + a
                    w = w_hi[:, s % RING, a * 2 * NGATE:(a + 1) * 2 * NGATE]
                    pe_.matmul(ps_x[0:2 * NGATE, 0:T], w, a_hi[:, kt, :], start=(kt == 0), stop=False)
                    last = pe_.matmul(ps_x[0:2 * NGATE, 0:T], w, a_lo[:, kt, :], start=False, stop=(kt == KD - 1))
                last.then_inc(granule_used, 1)
            pe_.wait_ge(evac_act, H_Q + 4)
            pe_.wait_ge(turned_copied, 14)
            transposes(1)
            pe_.wait_ge(gates_t_copied, 1)
            for j in range(NT):
                for part in range(2):
                    last = pe_.matmul(ps_x[:, T + j * NGATE:T + (j + 1) * NGATE], gates_t[:, j * P:(j + 1) * P],
                                      ident[0:2 * NGATE, part * NGATE:(part + 1) * NGATE],
                                      start=(part == 0), stop=(part == 1))
            last.then_inc(gate_turned, 1)
            for sec, h0 in enumerate((H_U, H_V)):
                with pe_.Fori(0, 2) as i:
                    for par in range(2):
                        pe_.wait_ge(evac_act, (h0 + par - 1) + 2 * i)
                        for s in range(SL):
                            granule((granule_of(h0 + par) + s) + 2 * SL * i, s % RING, par, s, SL, a_hi, a_lo)
                            attend(s, (4 * sec + par) + 2 * i, sec, par)
            for half in range(4):
                pe_.wait_ge(evac_act, H_ZB + half - 1)
                for s in range(SL):
                    granule(granule_of(H_ZB + half) + s, s % RING, half % 2, s, SL, a_hi, a_lo)
                    attend(s, 8 + half, 2, half % 2)
                    if half == 0 and MIX_SLOT <= s < MIX_SLOT + BG // 2:
                        m = s - MIX_SLOT
                        if m == 0:
                            pe_.wait_ge(gate_act, 2)
                            pe_.wait_ge(v_normed, 2)
                            pe_.wait_ge(sguw_masked, 1)
                        else:
                            pe_.wait_ge(mixed, 4 * m)
                        for q in range(4):
                            grp, j = 2 * m + q // 2, q % 2
                            last = pe_.matmul(ps_x[:, q * P:(q + 1) * P], sgu_wt[:, grp, :],
                                              v_b[:, j, grp * P:(grp + 1) * P], start=True, stop=True)
                        last.then_inc(gated, 1)
            with pe_.Fori(0, 2) as i:
                for par in range(2):
                    pe_.wait_ge(evac_act, (H_ZA + par - 1) + 2 * i)
                    for s in range(SL):
                        granule((granule_of(H_ZA + par) + s) + 2 * SL * i, s % RING, par, s, SL, a_hi, a_lo)
                        attend(s, (12 + par) + 2 * i, 3, par)

            for par in range(2):
                pe_.wait_ge(evac_act, H_M + par - 1)
                for s in range(SL):
                    granule(granule_of(H_M + par) + s, s % RING, par, s, SL, a_hi, a_lo)
                    q = SL * par + s
                    if q == 0:
                        pe_.wait_ge(z_used, 8)
                    if q == 16:
                        pe_.wait_ge(z_used, 16)
                    wait(pe_, o_lo_done, q - 1)
                    ps = ps_s if q % 2 == 0 else ps_t
                    for j in range(NT):
                        src = u_b[:, j, s * P:(s + 1) * P] if par == 0 else q_o[:, s, j * DH:(j + 1) * DH]
                        last = pe_.transpose(ps[:, j * P:(j + 1) * P], src, ident[:])
                    last.then_inc(o_turned, 1)
            with pe_.Fori(1, D // NB) as i:
                for par in range(2):
                    pe_.wait_ge(m_act, 4 * i - 2 + 2 * par)
                    for s in range(SL):
                        granule((granule_of(H_M + par) + s) + 2 * SL * i, s % RING, par, s, SL, a_hi, a_lo)

            def turn_merged(c, q):
                pe_.wait_ge(merge_steps, 5 * c + 5)
                if q >= 2:
                    pe_.wait_ge(m_lo_done, 4 * c + q - 1)
                ps = ps_s if q % 2 == 0 else ps_t
                for j in range(NT):
                    last = pe_.transpose(ps[:, j * P:(j + 1) * P], merged[:, j, q * P:(q + 1) * P], ident[:])
                last.then_inc(m_turned, 1)

            def y_half(c, first_):
                for k, (hi, lo) in enumerate(((o_hi, o_lo), (b_hi, b_lo))):
                    if first_:
                        pe_.wait_ge(m_act, 4 * (D // NB) - 2 + 2 * k)
                    else:
                        pe_.wait_ge(merge_steps, 5 * c - 3 + 2 * k)
                    for s in range(YSL):
                        granule((granule_of(H_Y) + YSL * k + s) + 2 * YSL * c, s % RING, k, s, YSL, hi, lo)
                        if not first_ and k == 0 and 1 <= s < 5:
                            turn_merged(c - 1, s - 1)

            pe_.wait_ge(o_lo_done, 2 * AW // P)
            y_half(0, True)
            with pe_.Fori(1, D // NB) as c:
                y_half(c, False)

            def w_half(c, par, first_=False, n=SL):
                if first_:
                    pe_.wait_ge(merge_steps, 5 * (D // NB) - 3)
                for s in range(n):
                    if first_ and s == SL - 2:
                        pe_.wait_ge(m_lo_done, KD)
                    if first_ and s == 0:
                        pe_.wait_ge(m_lo_done, KD - 4)
                    granule((granule_of(H_W) + s) + SL * c, s % RING, par, s, SL, a_hi, a_lo)
                    if first_ and 1 <= s < 5:
                        turn_merged(D // NB - 1, s - 1)

            w_half(0, 0, True)
            pe_.wait_ge(merge_steps, 5 * (D // NB) - 1)
            w_half(1, 1)
            with pe_.Fori(1, D // NB // 2 - 1) as i:
                for par in range(2):
                    pe_.wait_ge(y_squared, 4 * i - 2 + 2 * par)
                    w_half(2 * i + par, par)
            for c in (D // NB - 2, D // NB - 1):
                pe_.wait_ge(y_squared, 2 * c - 2)
                w_half(c, c % 2, n=SL if c % 2 == 0 else SL - RING)
            last_granules()


GATE = (1, 2, 0)

_OUT = ((1, T, D), "float32")


def kernel(**inputs):
    import concourse.bacc as bacc
    from concourse.bass_utils import run_bass_kernel_spmd

    a = {k: np.asarray(v) for k, v in inputs.items()}
    arrays = {
        "x_nat": a["x"][0],
        "x_t": np.ascontiguousarray(a["x"][0].T),
        "rel_bias": a["rel_bias"],
        "pre_norm_t": np.ascontiguousarray(a["pre_norm"][0].reshape(KD, P).T),
        "w_in": a["w_in"][0],
        "pe_t": np.ascontiguousarray(np.stack([a["cmp_pe_k"][0].T, a["cmp_pe_v"][0].T])),
        "w1_k": a["cmp_w1_k"][0], "w2_k": a["cmp_w2_k"][0],
        "w1_v": a["cmp_w1_v"][0], "w2_v": a["cmp_w2_v"][0],
        "w_out_a": a["w_out_a"][0],
        "sgu_norm": a["sgu_norm"][0],
        "sgu_w_t": np.ascontiguousarray(a["sgu_w"][0].transpose(2, 0, 1)),
        "sgu_b_t": np.ascontiguousarray(a["sgu_b"][0].T),
        "w_out_b": a["w_out_b"][0],
        "w_out": a["w_out"][0],
        "post_norm": a["post_norm"][0],
        "select": selectors(),
        "any_valid": (np.arange(P) >= L_CMP - 1).astype(np.float32).reshape(P, 1),
    }
    nc = bacc.Bacc("TRN2", target_bir_lowering=False, num_devices=1)
    args = [nc.dram_tensor(f"in_{n}", v.shape, mybir.dt.from_np(v.dtype), kind="ExternalInput").ap()
            for n, v in arrays.items()]
    args.append(nc.dram_tensor("out_dram", _OUT[0], F32, kind="ExternalOutput").ap())
    layer_kernel(nc, *args)
    feeds = {f"in_{n}": np.ascontiguousarray(v) for n, v in arrays.items()}
    return run_bass_kernel_spmd(nc, [feeds], core_ids=[0]).results[0]["out_dram"]
```
